# Optimizing a Trainium2 kernel written in Bass

```python
import math
import jax, jax.numpy as jnp
from jax import lax
import numpy as np

D_MODEL = 2048
BATCH = 1
SEQ = 512
DEPTH = 1
DEC_BATCH = 8
DEC_SEQ = 8
PAST_LEN = 4096
PAGE_SIZE = 128

N_META = 16
MIX_WIDTH = D_MODEL
GDN_HEAD_DIM = 128
GDN_HEADS = (MIX_WIDTH // 2) // GDN_HEAD_DIM
GDN_KEY_W = GDN_HEADS * GDN_HEAD_DIM
GDN_VAL_W = GDN_HEADS * GDN_HEAD_DIM
HG_HEAD_DIM = 128
HG_EXPAND = 128
HG_HEADS = (MIX_WIDTH - GDN_VAL_W) // HG_HEAD_DIM
HG_KEY_W = HG_HEADS * HG_EXPAND
HG_VAL_W = HG_HEADS * HG_HEAD_DIM
CONV_W = 4
CHUNK = 64
D_FF = 4 * D_MODEL
EPS = 1e-6
SPLIT_SIZES = (GDN_KEY_W, GDN_KEY_W, GDN_VAL_W, GDN_VAL_W, GDN_HEADS, GDN_HEADS,
               HG_KEY_W, HG_KEY_W, HG_VAL_W, HG_VAL_W)
N_IN = 2 * GDN_KEY_W + 2 * GDN_VAL_W + 2 * GDN_HEADS + 2 * HG_KEY_W + 2 * HG_VAL_W

kernel_name = "hymba_gdn_hgrn2_decoder_step"

def rmsnorm(x, w):
    xf = x.astype(jnp.float32)
    y = xf * lax.rsqrt(jnp.mean(xf * xf, axis=-1, keepdims=True) + EPS)
    return (y * w.astype(jnp.float32)).astype(x.dtype)

def l2norm(x):
    return x * lax.rsqrt(jnp.sum(x * x, axis=-1, keepdims=True) + EPS)

def gated_head_norm(o, z, w):
    y = o * lax.rsqrt(jnp.mean(o * o, axis=-1, keepdims=True) + EPS)
    return y * w.astype(jnp.float32) * jax.nn.silu(z.astype(jnp.float32))

def causal_conv(u, buf, w):
    full = jnp.concatenate([buf.astype(u.dtype), u], axis=1)
    C = u.shape[-1]
    out = lax.conv_general_dilated(full, w.astype(u.dtype)[:, None, :], window_strides=(1,),
                                   padding='VALID', dimension_numbers=('NWC', 'WIO', 'NWC'),
                                   feature_group_count=C)
    return jax.nn.silu(out), full[:, -(CONV_W - 1):]

def _chunks(t, chunk):
    B, L = t.shape[:2]
    t = t.reshape((B, L // chunk, chunk) + t.shape[2:])
    perm = (1, 0, 3, 2) + tuple(range(4, t.ndim))
    return t.transpose(perm)

def _unchunk(t):
    n, B, H, C, V = t.shape
    return t.transpose(1, 0, 3, 2, 4).reshape(B, n * C, H, V)

def gdn_chunked(q, k, v, beta, g, S0, chunk):
    V = v.shape[-1]
    incl = jnp.tril(jnp.ones((chunk, chunk), bool))
    strict = jnp.tril(jnp.ones((chunk, chunk), bool), -1)
    eye = jnp.eye(chunk, dtype=jnp.float32)

    def step(S, xs):
        qc, kc, vc, bc, gc = xs
        b = jnp.cumsum(gc, axis=-1)
        diff = b[..., :, None] - b[..., None, :]
        decay = jnp.exp(jnp.where(incl, diff, -jnp.inf))
        kb = kc * bc[..., None]
        A = jnp.where(strict, jnp.einsum('bhtk,bhsk->bhts', kb, kc) * decay, 0.0)
        rhs = jnp.concatenate([vc * bc[..., None], kb * jnp.exp(b)[..., None]], axis=-1)
        sol = lax.linalg.triangular_solve(A + eye, rhs, left_side=True, lower=True,
                                          unit_diagonal=True)
        U, W = sol[..., :V], sol[..., V:]
        v_new = U - jnp.einsum('bhck,bhkv->bhcv', W, S)
        qk = jnp.einsum('bhtk,bhsk->bhts', qc, kc) * decay
        o = (jnp.einsum('bhck,bhkv->bhcv', qc * jnp.exp(b)[..., None], S)
             + jnp.einsum('bhts,bhsv->bhtv', qk, v_new))
        bl = b[..., -1:]
        S_new = (jnp.exp(bl)[..., None] * S
                 + jnp.einsum('bhck,bhcv->bhkv', kc * jnp.exp(bl - b)[..., None], v_new))
        return S_new, o

    xs = (_chunks(q, chunk), _chunks(k, chunk), _chunks(v, chunk),
          _chunks(beta, chunk), _chunks(g, chunk))
    S, o = lax.scan(step, S0, xs)
    return S, _unchunk(o)

def hgrn2_chunked(q, k, v, g, S0, chunk):
    incl = jnp.tril(jnp.ones((chunk, chunk), bool))[..., None]

    def step(S, xs):
        qc, kc, vc, gc = xs
        b = jnp.cumsum(gc, axis=-2)
        diff = b[..., :, None, :] - b[..., None, :, :]
        decay = jnp.exp(jnp.where(incl, diff, -jnp.inf))
        A = jnp.einsum('bhtk,bhsk,bhtsk->bhts', qc, kc, decay)
        o = (jnp.einsum('bhck,bhkv->bhcv', qc * jnp.exp(b), S)
             + jnp.einsum('bhts,bhsv->bhtv', A, vc))
        bl = b[..., -1:, :]
        S_new = (jnp.exp(bl[..., 0, :])[..., None] * S
                 + jnp.einsum('bhck,bhcv->bhkv', kc * jnp.exp(bl - b), vc))
        return S_new, o

    xs = (_chunks(q, chunk), _chunks(k, chunk), _chunks(v, chunk), _chunks(g, chunk))
    S, o = lax.scan(step, S0, xs)
    return S, _unchunk(o)

def token_mixer(h, conv_buf, s_gdn, s_hg, lb, w_in, conv_w, a_log, dt_bias,
                gdn_norm_w, hg_norm_w, w_out, segments):
    B, L, _ = h.shape
    f32 = jnp.float32
    proj = h @ w_in
    parts, off = [], 0
    for s in SPLIT_SIZES:
        parts.append(proj[..., off:off + s])
        off += s
    qg, kg, vg, zg, bg, ag, qh, fh, ih, zh = parts
    qkv, new_buf = causal_conv(jnp.concatenate([qg, kg, vg], axis=-1), conv_buf, conv_w)
    qkv = qkv.astype(f32)
    q = l2norm(qkv[..., :GDN_KEY_W].reshape(B, L, GDN_HEADS, GDN_HEAD_DIM)) * (GDN_HEAD_DIM ** -0.5)
    k = l2norm(qkv[..., GDN_KEY_W:2 * GDN_KEY_W].reshape(B, L, GDN_HEADS, GDN_HEAD_DIM))
    v = qkv[..., 2 * GDN_KEY_W:].reshape(B, L, GDN_HEADS, GDN_HEAD_DIM)
    beta = jax.nn.sigmoid(bg.astype(f32))
    g = -jnp.exp(a_log.astype(f32)) * jax.nn.softplus(ag.astype(f32) + dt_bias.astype(f32))
    fgate = lb + (1.0 - lb) * jax.nn.sigmoid(fh.astype(f32))
    gh = jnp.log(fgate).reshape(B, L, HG_HEADS, HG_EXPAND)
    kh = (1.0 - fgate).reshape(B, L, HG_HEADS, HG_EXPAND)
    qhh = qh.astype(f32).reshape(B, L, HG_HEADS, HG_EXPAND)
    vh = ih.astype(f32).reshape(B, L, HG_HEADS, HG_HEAD_DIM)
    s_gdn = s_gdn.astype(f32)
    s_hg = s_hg.astype(f32)
    og_list, oh_list, start = [], [], 0
    for length, chunk in segments:
        sl = slice(start, start + length)
        s_gdn, o1 = gdn_chunked(q[:, sl], k[:, sl], v[:, sl], beta[:, sl], g[:, sl], s_gdn, chunk)
        s_hg, o2 = hgrn2_chunked(qhh[:, sl], kh[:, sl], vh[:, sl], gh[:, sl], s_hg, chunk)
        og_list.append(o1)
        oh_list.append(o2)
        start += length
    og = gated_head_norm(jnp.concatenate(og_list, axis=1),
                         zg.reshape(B, L, GDN_HEADS, GDN_HEAD_DIM), gdn_norm_w)
    oh = gated_head_norm(jnp.concatenate(oh_list, axis=1),
                         zh.reshape(B, L, HG_HEADS, HG_HEAD_DIM), hg_norm_w)
    mix = jnp.concatenate([og.reshape(B, L, GDN_VAL_W), oh.reshape(B, L, HG_VAL_W)],
                          axis=-1).astype(h.dtype)
    return mix @ w_out, new_buf, s_gdn, s_hg

def run_trunk(x, conv_st, gdn_st, hg_st, segments, norm1_w, w_in, conv_w, a_log, dt_bias,
              gdn_norm_w, hgrn_lb, hgrn_norm_w, w_out, norm2_w, w_up, w_down, final_norm_w):
    p = jax.nn.softmax(hgrn_lb.astype(jnp.float32), axis=0)
    lb_all = jnp.cumsum(p, axis=0) - p[0]
    new_conv, new_gdn, new_hg = [], [], []
    for l in range(DEPTH):
        h = rmsnorm(x, norm1_w[l])
        mix, c, sg, sh = token_mixer(h, conv_st[l], gdn_st[l], hg_st[l], lb_all[l], w_in[l],
                                     conv_w[l], a_log[l], dt_bias[l], gdn_norm_w[l],
                                     hgrn_norm_w[l], w_out[l], segments)
        x = x + mix
        u = jax.nn.relu(rmsnorm(x, norm2_w[l]) @ w_up[l])
        x = x + (u * u) @ w_down[l]
        new_conv.append(c)
        new_gdn.append(sg)
        new_hg.append(sh)
    return (rmsnorm(x, final_norm_w), jnp.stack(new_conv), jnp.stack(new_gdn), jnp.stack(new_hg))

def setup_inputs(seed: int = 0) -> dict:
    key = jax.random.key(seed)
    ks = jax.random.split(key, 20)
    f32 = jnp.float32
    nrm = lambda k, shape, s: jax.random.normal(k, shape, f32) * s
    dt = jnp.exp(jax.random.uniform(ks[9], (DEPTH, GDN_HEADS), f32)
                 * (math.log(0.1) - math.log(0.001)) + math.log(0.001))
    return {
        "x_prompt": nrm(ks[0], (BATCH, SEQ, D_MODEL), 1.0),
        "x_sample": nrm(ks[1], (DEC_BATCH, DEC_SEQ, D_MODEL), 1.0),
        "state_gdn_conv": nrm(ks[2], (DEPTH, DEC_BATCH, CONV_W - 1, 3 * GDN_KEY_W), 1.0),
        "state_gdn": nrm(ks[3], (DEPTH, DEC_BATCH, GDN_HEADS, GDN_HEAD_DIM, GDN_HEAD_DIM), 0.1),
        "state_hgrn": nrm(ks[4], (DEPTH, DEC_BATCH, HG_HEADS, HG_EXPAND, HG_HEAD_DIM), 0.5),
        "meta_tokens": nrm(ks[5], (N_META, D_MODEL), 1.0),
        "norm1_w": 1.0 + nrm(ks[6], (DEPTH, D_MODEL), 0.02),
        "w_in": nrm(ks[7], (DEPTH, D_MODEL, N_IN), D_MODEL ** -0.5),
        "conv_w": nrm(ks[8], (DEPTH, CONV_W, 3 * GDN_KEY_W), 0.5),
        "a_log": jnp.log(jax.random.uniform(ks[10], (DEPTH, GDN_HEADS), f32, 1.0, 16.0)),
        "dt_bias": dt + jnp.log(-jnp.expm1(-dt)),
        "gdn_norm_w": 1.0 + nrm(ks[11], (DEPTH, GDN_HEAD_DIM), 0.02),
        "hgrn_lb": nrm(ks[12], (DEPTH, HG_KEY_W), 0.1),
        "hgrn_norm_w": 1.0 + nrm(ks[13], (DEPTH, HG_HEAD_DIM), 0.02),
        "w_out": nrm(ks[14], (DEPTH, MIX_WIDTH, D_MODEL), MIX_WIDTH ** -0.5),
        "norm2_w": 1.0 + nrm(ks[15], (DEPTH, D_MODEL), 0.02),
        "w_up": nrm(ks[16], (DEPTH, D_MODEL, D_FF), D_MODEL ** -0.5),
        "w_down": nrm(ks[17], (DEPTH, D_FF, D_MODEL), D_FF ** -0.5),
        "final_norm_w": 1.0 + nrm(ks[18], (D_MODEL,), 0.02),
    }

def reference(x_prompt, x_sample, state_gdn_conv, state_gdn, state_hgrn, meta_tokens, norm1_w,
              w_in, conv_w, a_log, dt_bias, gdn_norm_w, hgrn_lb, hgrn_norm_w, w_out, norm2_w,
              w_up, w_down, final_norm_w):
    B = x_prompt.shape[0]
    xp = jnp.concatenate([jnp.broadcast_to(meta_tokens.astype(x_prompt.dtype)[None],
                                           (B, N_META, D_MODEL)), x_prompt], axis=1)
    zc = jnp.zeros((DEPTH, B, CONV_W - 1, 3 * GDN_KEY_W), x_prompt.dtype)
    zg = jnp.zeros((DEPTH, B, GDN_HEADS, GDN_HEAD_DIM, GDN_HEAD_DIM), jnp.float32)
    zh = jnp.zeros((DEPTH, B, HG_HEADS, HG_EXPAND, HG_HEAD_DIM), jnp.float32)
    yp, pc, pg, ph = run_trunk(xp, zc, zg, zh, [(N_META, N_META), (SEQ, CHUNK)], norm1_w, w_in,
                               conv_w, a_log, dt_bias, gdn_norm_w, hgrn_lb, hgrn_norm_w, w_out,
                               norm2_w, w_up, w_down, final_norm_w)
    ys, sc, sg, sh = run_trunk(x_sample, state_gdn_conv, state_gdn, state_hgrn,
                               [(DEC_SEQ, DEC_SEQ)], norm1_w, w_in, conv_w, a_log, dt_bias,
                               gdn_norm_w, hgrn_lb, hgrn_norm_w, w_out, norm2_w, w_up, w_down,
                               final_norm_w)
    return (yp[:, N_META:], ys, pc.astype(x_prompt.dtype), pg.astype(state_gdn.dtype),
            ph.astype(state_hgrn.dtype), sc.astype(state_gdn_conv.dtype),
            sg.astype(state_gdn.dtype), sh.astype(state_hgrn.dtype))


_drawn_inputs = setup_inputs


def setup_inputs(seed=0):
    import zlib

    import numpy as np

    out = dict(_drawn_inputs(seed))
    spreads = {}
    factors = {'gdn_norm_w': 6.81, 'hgrn_norm_w': 6.804, 'norm2_w': 3.26, 'final_norm_w': 2.834}
    for name, (base, spread) in spreads.items():
        noise = np.random.default_rng([zlib.crc32(name.encode()), seed]).standard_normal(out[name].shape)
        drawn = base * np.exp(spread * noise) if base else spread * noise
        out[name] = __import__('jax').numpy.asarray(drawn.astype(out[name].dtype))
    for name, factor in factors.items():
        out[name] = (out[name] * factor).astype(out[name].dtype)
    return out
```

```python
from contextlib import ExitStack

import concourse.bass as bass
from concourse import mybir

F32 = mybir.dt.float32
F32R = mybir.dt.float32r
U8 = mybir.dt.uint8
ALU = mybir.AluOpType
ACT = mybir.ActivationFunctionType
AX = mybir.AxisListType

P = 128
D = 2048
KT = D // P
SB, ST = 8, 8
NS, NM, NP_ = SB * ST, 16, 512
T0 = NS + NM
N = T0 + NP_
HALF = N // 2
NW = 5
HEADS = 8
N_IN = 8208
DFF = 4 * D
GK = HEADS * P
HG0 = 4 * GK + 2 * HEADS
TAPS = 4
PRE = TAPS - 1
USEQ = PRE + ST
UP0 = SB * USEQ
UW = UP0 + PRE + NM + NP_
CW = UW - PRE
UK = 8
RAW = 4
EPS = 1e-6
BIG = 1e18
LEVELS = [1, 2, 4, 8, 16, 32, 64]
FG = 8
GROUPS = DFF // P // FG

IN_UNITS = 2 + 16 * HEADS
OUT_U0 = IN_UNITS
MLP_U0 = OUT_U0 + 2 * KT
GU = 2 * FG + KT
OUT_T0 = 1 + 8 * HEADS
MLP_T0 = OUT_T0 + KT
GT = FG + KT
LAST_UP = MLP_U0 + GU * (GROUPS - 1) + 2 * FG


def w0(c):
    return 0 if c == 0 else T0 + P * (c - 1)


def wn(c):
    return T0 if c == 0 else P


MASK_STEPS = 5 + 2 + 2 + 4 + 5 + 4 + 1 + len(LEVELS) * (3 + NW) + NW + 3


def settle(eng, spare, steps, name, h):
    i = steps.names.index(name)
    if i or not isinstance(h, int) or h:
        eng.wait_ge(steps.sem, h * steps.n + i)
    steps.done(eng.tensor_tensor(spare[:, 0:1], spare[:, 1:2], spare[:, 1:2], ALU.add), name)


class Steps:

    def __init__(self, sem, names):
        self.sem, self.names, self.n = sem, list(names), len(names)
        self.next = 0
        assert len(set(self.names)) == self.n

    def done(self, ins, name):
        assert self.names[self.next % self.n] == name, (self.names[self.next % self.n], name)
        self.next += 1
        ins.then_inc(self.sem, 1)

    def wait(self, eng, name, h):
        eng.wait_ge(self.sem, h * self.n + (self.names.index(name) + 1))


def spread(stages, first, last):
    n = len(stages)
    return {s: first + (i * (last - first)) // max(n - 1, 1) for i, s in enumerate(stages)}


INV = [b for b in LEVELS if b > 1]
T_STEPS = [f"{s}{b}" for b in INV[:-1] for s in ("p", "tp", "t")]
GDN_STAGES = {"gates": 0, "norms": 14, "rows": 15, "scores": 20, "turn_v": 21, "turn_k": 22, "ws0": 23, "turn_r0": 24,
              **spread(["t1"] + T_STEPS + ["p64", "tp64", "vn0", "st0"]
                       + [f"{s}_{c}" for c in range(1, NW) for s in ("ws", "vn", "st")] + ["out"], 25, 63)}
HG_STAGES = {"gates": 1, "conv_in": 6, "turn_v": 8, "turn_k": 18, "stw": 20, "diag": 22,
             **spread([f"l{b}" for b in LEVELS] + ["o", "st0", "out"], 24, 58)}

START_PE = ["conv_rows", "vec_rows"] + [f"turn{k}" for k in range(KT)] + ["rstd", "cols"]
START_ACT = ["ln", "exp", "a", "lb", "b_exp", "b_ln", "b_sig", "s_exp", "s_ln", "e_exp"]
START_DVE = ["params", "ssq0"] + [f"x{k}" for k in range(KT)] + ["ssum", "diag", "rstd", "lb0", "lb1", "lb2", "lb3",
             "one_lb", "dt", "clamp", "abs", "soft", "g", "b", "e_arg", "cols"]
GDN_PE = (["conv_in", "conv_out", "norms", "rows", "scores", "turn_v", "turn_k", "ws0", "turn_r0", "t1"] + T_STEPS
          + ["p64", "tp64", "vn0", "o0", "st0"] + [f"{s}_{c}" for c in range(1, NW) for s in ("ws", "vn", "st", "o")]
          + ["out"])
GDN_ACT = (["conv_out", "exp", "ln", "sig", "zexp", "zln", "zsig", "square", "rln", "rexp", "brow", "eb", "decay",
            "vt", "r0", "t1"] + [f"{s}{b}" for b in INV[:-1] for s in ("p", "t")] + ["p64", "vn0", "o0"]
           + [f"{s}_{c}" for c in range(1, NW) for s in ("vn", "o")] + ["osq", "oln", "oexp"])
GDN_DVE = (["conv_in", "conv_0", "conv_1", "conv_2", "last", "sel", "clamp", "zclamp", "qkv", "zs", "qn", "kn", "kb",
            "vb", "diff", "keb", "qe", "dm", "at", "qkd", "tt0", "tt1", "kd", "r0"] + [f"t{b}" for b in INV[:-1]]
           + ["tt64", "vx", "sb_scale", "sb", "sc_0"] + [f"{s}_{c}" for c in range(1, NW) for s in ("r", "sc")]
           + ["y1", "y"])
GDN_POOL = [f"x{b}" for b in INV]
HG_PE = ["turn_v", "turn_k", "stw", "diag"] + [f"l{b}" for b in LEVELS] + ["o0", "o", "st0", "out"]
HG_ACT = (["exp", "zexp", "ln", "lnlb", "sig", "zln", "zsig", "eb", "kdexp", "vt"] + [f"e{b}" for b in LEVELS]
          + ["o0", "o", "osq", "oln", "oexp"])
LEVEL_DVE = ["arg1"] + [s for b in LEVELS for s in (([f"arg{b}", f"a{b // 2}"] if b > 1 else []) + [f"q{b}", f"kk{b}"])] + ["a64"]
HG_DVE = (["clamp", "zclamp", "g", "k0", "k", "b", "zs", "kdarg", "qe", "kd", "vx", "kdt", "sc_0"]
          + [f"sc_{c}" for c in range(1, NW)] + ["diag"] + LEVEL_DVE
          + ["sb_scale", "sb", "y1", "y"])
HG_POOL = ["zero"]


def hymba_kernel(nc, io):
    ctx = ExitStack()
    with ctx:
        def sb(name, shape, dt=F32, stack=ctx):
            return stack.enter_context(nc.sbuf_tensor(name, shape, dt))

        def sem(name):
            return ctx.enter_context(nc.semaphore(name))

        xT_dram = nc.dram_tensor("xT_scratch", [D, N], F32, kind="Internal").ap().rearrange("(k p) n -> p k n", p=P)
        mix_dram = nc.dram_tensor("mix_scratch", [D, N], F32, kind="Internal").ap().rearrange("(k p) n -> p k n", p=P)

        with ExitStack() as s:
            y = sb("y", [P, NW, D], stack=s)
            final_w = sb("final_w", [P, D], stack=s)
        h_hi = sb("h_hi", [P, KT, N], F32R)
        h_lo = sb("h_lo", [P, KT, N], F32R)
        w_raw = sb("w_raw", [P, RAW, UK, P])
        w_hi = sb("w_hi", [P, 2, UK, P], F32R)
        w_lo = sb("w_lo", [P, 2, UK, P], F32R)
        ident = sb("ident", [P, P])
        ones = sb("ones", [P, P])
        conv_w = sb("conv_w_t", [P, TAPS, 3, HEADS])
        vecs = sb("vecs_t", [P, 2 * KT + HEADS + 2])
        norm2_w, lb_raw = vecs[:, KT:2 * KT], vecs[:, 2 * KT:2 * KT + HEADS]
        gdn_w, hg_w = (vecs[:, 2 * KT + HEADS + i:2 * KT + HEADS + i + 1] for i in range(2))
        eps = sb("eps", [P, 1])
        pool_spare, dve_spare = sb("pool_spare", [1, 4]), sb("dve_spare", [1, 2])
        rstd = sb("rstd", [P, N])

        with ExitStack() as s:
            x_tok = sb("x_tok", [P, NW, D], stack=s)
            xT = sb("xT", [P, KT, N], stack=s)
            conv_rows = sb("conv_rows", [TAPS * 3 * HEADS, P], stack=s)
            vec_rows = sb("vec_rows", [2 * KT + HEADS + 2, P], stack=s)
            ssq = sb("ssq", [P, NW, 4], stack=s)
            ssum = sb("ssum", [P, NW], stack=s)
            sq_dump = sb("sq_dump", [P, 512], stack=s)
            diag = sb("diag", [P, NW, P], stack=s)
        with ExitStack() as s:
            masks = sb("masks", [P, len(LEVELS), P], stack=s)
            pmask = sb("pmask", [P, len(LEVELS), NW * 64], U8, stack=s)
            imask = sb("imask", [P, NW, P], U8, stack=s)
            causal = sb("causal", [P, NW, P], stack=s)
            seq_rows = sb("seq_rows", [P, SB + 1], stack=s)
            run = sb("run", [P, N], stack=s)
            beta_rows = sb("beta_rows", [16, N], stack=s)
            b_rows = sb("b_rows", [16, N], stack=s)
            one_hot = sb("one_hot", [16, 16], stack=s)
            dt_bias = sb("dt_bias_c", [16, 1], stack=s)
            a_exp = sb("a_exp", [16, 1], stack=s)
            b_col = sb("b_col", [P, NW, 16], stack=s)
            e_col = sb("e_col", [P, NW, 16], stack=s)
            lb = sb("lb", [P, HEADS], stack=s)
            one_lb = sb("one_lb", [P, HEADS], stack=s)
            lb_tmp = sb("lb_tmp", [P, 2, HEADS], stack=s)
            u = sb("u", [P, 3, UW], stack=s)
            gz = sb("gz", [P, N], stack=s)
            hq, hf, hv, hz = (sb(n, [P, N], stack=s) for n in ("hq", "hf", "hv", "hz"))
            hist_in = sb("hist_in", [P, 3, P], stack=s)
            last = sb("last", [P, 3, (SB + 1) * PRE], stack=s)
            hist_out = sb("hist_out", [(SB + 1) * PRE, 3, P], stack=s)
            state = sb("state", [P, SB, P], stack=s)
            tmp = sb("tmp", [P, 12200], stack=s)
        top = [0]

        def at(*shape):
            n = 1
            for d in shape:
                n *= d
            v = tmp[:, top[0]:top[0] + n]
            top[0] += n
            assert top[0] <= 12200
            return v if len(shape) == 1 else v.rearrange("p (a b) -> p a b", a=shape[0])

        conv = at(3, CW)
        gate = at(3, CW)
        qkv = at(3, N)
        rs = at(2, N)
        aT, qkd, xl, tm, tT = (at(NW, P) for _ in range(5))
        pc = at(NW, 64)
        vbt = at(4, P)
        kdt = at(NW, P)
        r0T, r, vn = at(P), at(P), at(P)
        sc = at(2, P)
        decay = tm
        gze = xl.rearrange("p a b -> p (a b)")[:, 0:N]
        conv_f = conv.rearrange("p a b -> p (a b)")
        gate_f = gate.rearrange("p a b -> p (a b)")
        b_row, eb, qe = (conv_f[:, i * N:i * N + N] for i in range(3))
        kb, vb, keb = (gate_f[:, i * N:i * N + N] for i in range(3))
        vx = gate_f[:, 0:(SB + 1) * P].rearrange("p (a b) -> p a b", a=SB + 1)
        sel = [tT.rearrange("p a b -> p (a b)")[0:16, 0:N], kdt.rearrange("p a b -> p (a b)")[0:16, 0:N]]
        go = qkv[:, 0, :]
        top[0] = 3 * CW
        hl, hb, hk, heb, hkd, h_arg, hkk, ho, hqe = (at(N) for _ in range(9))
        hqq = at(HALF)
        hvt, hkdt, ha, hsc = (at(NW, P) for _ in range(4))
        hvx = at(SB + 1, P)
        bag, bag1, bag2 = (conv_f[0:16, i * N:i * N + N] for i in range(3))

        with ExitStack() as s:
            x1 = sb("x1", [P, KT, N], stack=s)
            relu = sb("relu", [P, 2, N], stack=s)
            relu2 = sb("relu2", [P, N], stack=s)
            with ExitStack() as s2:
                mix_in = sb("mix_in", [P, 4, N], stack=s2)
                sq = sb("sq", [P, 2, N], stack=s2)
                sq_sum = sb("sq_sum", [P, N], stack=s2)
            u_hi = sb("u_hi", [P, FG, N], F32R, stack=s)
            u_lo = sb("u_lo", [P, FG, N], F32R, stack=s)
            fin = sb("fin", [P, 2 * NW], stack=s)

        main = [ctx.enter_context(nc.psum_tensor(f"main{i}", [P, 2, 512], F32)) for i in range(2)]
        mx = ctx.enter_context(nc.psum_tensor("mx", [P, 4, 512], F32))
        mxf = mx[:, :, :].rearrange("p b n -> p (b n)")

        def mains(t):
            return main[t % 2][:, :, 0:HALF]

        s_x = [sem(f"x_loaded{i}") for i in range(4)]
        s_small = sem("small_loaded")
        s_w = [sem(f"weights_loaded{i}") for i in range(RAW)]
        s_hi = sem("weights_hi")
        s_lo = sem("weights_lo")
        s_unit = sem("unit_done")
        s_evac = sem("tile_evacuated")
        s_k_hi = sem("operand_hi")
        s_k_lo = sem("operand_lo")
        s_mask = sem("masks_built")
        s_spill = sem("xT_spilled")
        s_hist = sem("history_loaded")
        s_hist_out = sem("history_stored")
        s_gst = sem("gdn_state_loaded")
        s_gst_out = sem("gdn_state_stored")
        s_gsc_out = sem("gdn_prompt_state_stored")
        s_hst = sem("hgrn_state_loaded")
        s_hst_out = sem("hgrn_state_stored")
        s_hsc_out = sem("hgrn_prompt_state_stored")
        s_gmix = sem("gdn_mix_stored")
        s_hmix = sem("hgrn_mix_stored")
        s_mixin = [sem(f"mix_loaded{i}") for i in range(4)]
        s_xT = sem("xT_loaded")
        s_sq = sem("square_made")
        s_sqs = sem("square_summed")
        s_n2 = sem("norm2_sum")
        s_n2l = sem("norm2_rstd")
        s_tap = sem("conv_tap")
        s_dump = sem("x_squared")
        s_relu2 = sem("relu2_made")
        s_uhi = sem("u_hi_made")
        s_ulo = sem("u_lo_made")
        s_fin_pe = sem("final_turned")
        s_fin_copy = sem("final_copied")
        s_fin = sem("final_stats")
        s_fin_dve = sem("final_scaled")
        s_out = sem("y_stored")
        s_fw = sem("final_w_loaded")

        gpe, gact, gdve, gpool = (Steps(sem("gdn_pe"), GDN_PE), Steps(sem("gdn_act"), GDN_ACT),
                                  Steps(sem("gdn_dve"), GDN_DVE), Steps(sem("gdn_pool"), GDN_POOL))
        hpe, hact, hdve = (Steps(sem("hg_pe"), HG_PE), Steps(sem("hg_act"), HG_ACT), Steps(sem("hg_dve"), HG_DVE))
        hpool = Steps(sem("hg_pool"), HG_POOL)
        gset = Steps(sem("gdn_traffic"), ["hist", "in", "hist_out", "sb", "sc", "y"])
        hset = Steps(sem("hg_traffic"), ["in", "zero", "sb", "sc", "y"])
        dset = Steps(sem("dve_settled"), ["diag"] + [f"l{b}" for b in LEVELS])
        cpe, cact, cdve = (Steps(sem("start_pe"), START_PE), Steps(sem("start_act"), START_ACT),
                           Steps(sem("start_dve"), START_DVE))

        w_in = io["w_in"][0].rearrange("(k p) n -> p k n", p=P)
        w_out = io["w_out"][0].rearrange("(k p) n -> p k n", p=P)
        w_up = io["w_up"][0].rearrange("(k p) n -> p k n", p=P)
        w_down = io["w_down"][0].rearrange("(k p) n -> p k n", p=P)
        block = ctx.enter_context(nc.Block())

        def seq(ap):
            return ap[:, 0:NS].rearrange("p (b t) -> p b t", b=SB)

        @block.sync
        def _(sp):
            xs, xm, xp = io["x_sample"].rearrange("b t d -> (b t) d"), io["meta_tokens"], io["x_prompt"][0]
            for q in range(4):
                cols = slice(512 * q, 512 * q + 512)
                sp.dma_start(x_tok[0:NS, 0, cols], xs[:, cols]).then_inc(s_x[q], 16)
                sp.dma_start(x_tok[NS:T0, 0, cols], xm[:, cols]).then_inc(s_x[q], 16)
                sp.dma_start(x_tok[:, 1:NW, cols], xp[:, cols].rearrange("(c p) d -> p c d", p=P)).then_inc(s_x[q], 16)

            def load(src, unit, ring):
                if not isinstance(unit, int) or unit >= RAW:
                    sp.wait_ge(s_lo, unit - RAW + 1)
                sp.dma_start(w_raw[:, ring], src).then_inc(s_w[ring], 16)

            for j in range(2):
                load(w_in[:, UK * j:UK * j + UK, 4 * GK:4 * GK + P], j, j)

            def head(h):
                for j in range(16):
                    col = (0 if j < 8 else HG0) + (j % 8) // 2 * GK
                    k0 = UK * (j % 2)
                    src = (w_in[:, k0:k0 + UK, col + h * P:col + h * P + P] if isinstance(h, int)
                           else w_in[:, k0:k0 + UK, bass.ds(h * P + col, P)])
                    load(src, h * 16 + (2 + j), (2 + j) % RAW)

            head(0)
            with sp.Fori(1, HEADS) as h:
                head(h)

            def out_pair(i):
                for j in range(4):
                    k0 = UK * (j % 2)
                    load(w_out[:, k0:k0 + UK, bass.ds(i * (2 * P) + (j // 2) * P, P)], i * 4 + (OUT_U0 + j),
                         (OUT_U0 + j) % RAW)

            with sp.Fori(0, KT // 2) as i:
                out_pair(i)
            with sp.Fori(0, GROUPS) as g:
                for j in range(2 * FG):
                    k0 = UK * (j % 2)
                    load(w_up[:, k0:k0 + UK, bass.ds(g * (FG * P) + (j // 2) * P, P)], g * GU + (MLP_U0 + j),
                         (MLP_U0 + j) % RAW)
                for m in range(KT):
                    load(w_down[:, bass.ds(g * FG, FG), m * P:m * P + P], g * GU + (MLP_U0 + 2 * FG + m),
                         (MLP_U0 + m) % RAW)

        @block.gpsimd
        def _(pool):
            step = [0]

            def built(ins):
                step[0] += 1
                ins.then_inc(s_mask, 1)
                pool.wait_ge(s_mask, step[0])

            def keep(ap, pattern, base, mult, op=ALU.is_ge, fill=0.0):
                built(pool.affine_select(out=ap, in_=ap, compare_op=op, fill=fill, base=base, pattern=pattern,
                                         channel_multiplier=mult))

            cw = io["conv_w"][0].rearrange("w (t p) -> (w t) p", p=P)
            pool.dma_start(conv_rows[:, :], cw).then_inc(s_small, 16)
            pool.dma_start(vec_rows[0:KT, :], io["norm1_w"][0].rearrange("(k p) -> k p", p=P)).then_inc(s_small, 16)
            pool.dma_start(vec_rows[KT:2 * KT, :], io["norm2_w"][0].rearrange("(k p) -> k p", p=P)).then_inc(s_small, 16)
            pool.dma_start(vec_rows[2 * KT:2 * KT + HEADS, :],
                           io["hgrn_lb"][0].rearrange("(k p) -> k p", p=P)).then_inc(s_small, 16)
            pool.dma_start(vec_rows[2 * KT + HEADS:2 * KT + HEADS + 1, :], io["gdn_norm_w"]).then_inc(s_small, 16)
            pool.dma_start(vec_rows[2 * KT + HEADS + 1:2 * KT + HEADS + 2, :], io["hgrn_norm_w"]).then_inc(s_small, 16)

            built(pool.memset(ident[:, :], 0.0))
            keep(ident[:, :], [[-1, P]], 0, 1, ALU.not_equal, 1.0)
            built(pool.memset(ones[:, :], 1.0))
            built(pool.memset(eps[:, :], EPS))
            built(pool.memset(pool_spare[:, :], 0.0))
            assert step[0] == 5

            for q in range(4):
                cdve.wait(pool, f"x{4 * q + 3}", 0)
                pool.dma_start(xT_dram[:, 4 * q:4 * q + 4, :], xT[:, 4 * q:4 * q + 4, :]).then_inc(s_spill, 16)
            pool.wait_ge(s_spill, 16 * 4)
            pool.wait_ge(s_k_lo, KT)
            cdve.wait(pool, "rstd", 0)
            cpe.wait(pool, "rstd", 0)
            built(pool.memset(dt_bias[:, :], 0.0))
            built(pool.memset(a_exp[:, :], 0.0))
            pool.dma_start(dt_bias[HEADS:16, :], io["dt_bias"].rearrange("a n -> n a")).then_inc(s_small, 16)
            pool.dma_start(a_exp[HEADS:16, :], io["a_log"].rearrange("a n -> n a")).then_inc(s_small, 16)
            built(pool.memset(one_hot[:, :], 0.0))
            keep(one_hot[:, :], [[-1, 16]], 0, 1, ALU.not_equal, 1.0)
            built(pool.memset(run[:, :], 1.0))
            built(pool.memset(seq(run)[:, :, 0:1], 0.0))
            built(pool.memset(run[:, NS:NS + 1], 0.0))
            built(pool.memset(run[:, T0:N].rearrange("p (c t) -> p c t", c=4)[:, :, 0:1], 0.0))
            built(pool.memset(causal[:, :, :], 1.0))
            keep(causal[:, :, :], [[0, NW], [1, P]], 0, -1)
            keep(causal[:, 0, 0:NS].rearrange("p (b t) -> p b t", b=SB), [[-ST, SB], [0, ST]], 0, 1)
            keep(causal[:, 0, NS:T0], [[0, NM]], -NS, 1)
            built(pool.memset(causal[:, 0, T0:P], 0.0))
            built(pool.memset(seq_rows[:, :], 1.0))
            keep(seq_rows[:, :], [[-ST, SB + 1]], 0, 1)
            keep(seq_rows[:, 0:SB], [[ST, SB]], ST - 1, -1)
            keep(seq_rows[:, SB:SB + 1], [[0, 1]], T0 - 1, -1)
            built(pool.memset(masks[:, :, :], 0.0))
            for i, b in enumerate(LEVELS):
                right = masks[:, i, :].rearrange("p (n t b) -> p n t b", t=2, b=b)[:, :, 1, :]
                built(pool.memset(right, 1.0))
                keep(right, [[-2 * b, 64 // b], [0, b]], 0, 1)
                keep(right, [[2 * b, 64 // b], [0, b]], b - 1, -1)
                for c in range(NW):
                    built(pool.tensor_copy(pmask[:, i, 64 * c:64 * c + 64].rearrange("p (n b) -> p n b", b=b), right))
            for c in range(NW):
                built(pool.tensor_copy(imask[:, c, :], ident[:, :]))
            built(pool.memset(u[:, :, :], 0.0))
            built(pool.memset(hist_in[:, :, :], 0.0))
            built(pool.memset(tmp[:, :], 0.0))
            assert step[0] == MASK_STEPS, step[0]

            hist = io["state_gdn_conv"][0].rearrange("b j n -> (b j) n").rearrange("r (t n) -> r t n", t=3)
            hist_s = io["conv_sample"][0].rearrange("b j n -> (b j) n").rearrange("r (t n) -> r t n", t=3)
            hist_p = io["conv_prompt"][0].rearrange("b j n -> (b j) n").rearrange("r (t n) -> r t n", t=3)

            def cols(ap, h):
                return ap[:, :, h * P:h * P + P] if isinstance(h, int) else ap[:, :, bass.ds(h * P, P)]

            def state_of(name, h):
                ap = io[name][0].rearrange("b h k v -> k b h v")
                return ap[:, :, h, :] if isinstance(h, int) else ap[:, :, bass.ds(h, 1), :].rearrange("k b h v -> k b (h v)")

            def state1_of(name, h):
                ap = io[name][0, 0].rearrange("h k v -> k h v")
                return ap[:, h, :] if isinstance(h, int) else ap[:, bass.ds(h, 1), :].rearrange("k h v -> k (h v)")

            def mixed(h, base):
                return (mix_dram[:, base + h, :] if isinstance(h, int)
                        else mix_dram[:, bass.ds(h + base, 1), :].rearrange("p k n -> p (k n)"))

            def hist_load(h, first):
                if not first:
                    gpe.wait(pool, "conv_in", h - 1)
                settle(pool, pool_spare[:, 0:2], gset, "hist", h)
                pool.dma_start(hist_in[0:SB * PRE, :, :], cols(hist, h)).then_inc(s_hist, 16)

            def gdn_in(h, first):
                if not first:
                    pool.wait_ge(s_hst_out, h * 16)
                settle(pool, pool_spare[:, 0:2], gset, "in", h)
                pool.dma_start(state[:, :, :], state_of("state_gdn", h)).then_inc(s_gst, 16)

            def hg_in(h):
                pool.wait_ge(s_gst_out, h * 16 + 16)
                settle(pool, pool_spare[:, 2:4], hset, "in", h)
                pool.dma_start(state[:, :, :], state_of("state_hgrn", h)).then_inc(s_hst, 16)

            def gdn_side(h, first):
                gact.wait(pool, "conv_out", h)
                settle(pool, pool_spare[:, 0:2], gset, "hist_out", h)
                pool.dma_start(cols(hist_s, h), hist_out[0:SB * PRE, :, :]).then_inc(s_hist_out, 16)
                pool.dma_start(cols(hist_p, h), hist_out[SB * PRE:, :, :]).then_inc(s_hist_out, 16)
                gdve.wait(pool, "at", h)
                for b in INV:
                    if b == 2:
                        if not first:
                            gpe.wait(pool, "p64", h - 1)
                    else:
                        gpe.wait(pool, f"p{b // 2}", h)
                    i = LEVELS.index(b)
                    gpool.done(pool.tensor_tensor(xl[:, :, :], aT[:, :, :],
                                                  masks[:, i:i + 1, :].to_broadcast([P, NW, P]), ALU.mult), f"x{b}")
                gdve.wait(pool, "sb", h)
                settle(pool, pool_spare[:, 0:2], gset, "sb", h)
                pool.dma_start(state_of("gdn_sample", h), state[:, :, :]).then_inc(s_gst_out, 16)
                gdve.wait(pool, f"sc_{NW - 1}", h)
                settle(pool, pool_spare[:, 0:2], gset, "sc", h)
                pool.dma_start(state1_of("gdn_prompt", h), sc[:, 0, :]).then_inc(s_gsc_out, 16)
                gdve.wait(pool, "y", h)
                settle(pool, pool_spare[:, 0:2], gset, "y", h)
                pool.dma_start(mixed(h, 0), go[:, :]).then_inc(s_gmix, 16)

            def hg_side(h):
                gdve.wait(pool, "y", h)
                pool.wait_ge(s_gmix, h * 16 + 16)
                pool.wait_ge(s_gsc_out, h * 16 + 16)
                settle(pool, pool_spare[:, 2:4], hset, "zero", h)
                hpool.done(pool.memset(ha, 0.0), "zero")
                hdve.wait(pool, "sb", h)
                settle(pool, pool_spare[:, 2:4], hset, "sb", h)
                pool.dma_start(state_of("hgrn_sample", h), state[:, :, :]).then_inc(s_hst_out, 16)
                hdve.wait(pool, f"sc_{NW - 1}", h)
                settle(pool, pool_spare[:, 2:4], hset, "sc", h)
                pool.dma_start(state1_of("hgrn_prompt", h), hsc[:, NW - 1, :]).then_inc(s_hsc_out, 16)
                hdve.wait(pool, "y", h)
                settle(pool, pool_spare[:, 2:4], hset, "y", h)
                pool.dma_start(mixed(h, HEADS), ho[:, :]).then_inc(s_hmix, 16)

            hist_load(0, True)
            gdn_in(0, True)
            gdn_side(0, True)
            with pool.Fori(1, HEADS) as h:
                hist_load(h, False)
                hg_in(h - 1)
                hg_side(h - 1)
                gdn_in(h, False)
                gdn_side(h, False)
            hg_in(HEADS - 1)
            hg_side(HEADS - 1)

            pool.wait_ge(s_hist_out, 32 * HEADS)
            pool.wait_ge(s_gst_out, 16 * HEADS)
            pool.wait_ge(s_gsc_out, 16 * HEADS)
            pool.wait_ge(s_hst_out, 16 * HEADS)
            pool.wait_ge(s_hsc_out, 16 * HEADS)
            pool.wait_ge(s_gmix, 16 * HEADS)
            pool.wait_ge(s_hmix, 16 * HEADS)
            for k in range(KT):
                if k >= 4:
                    pool.wait_ge(s_k_lo, KT + k - 3)
                pool.dma_start(mix_in[:, k % 4, :], mix_dram[:, k, :]).then_inc(s_mixin[k % 4], 16)
            pool.dma_start(x1[:, :, :], xT_dram).then_inc(s_xT, 16)
            for m in range(KT):
                pool.wait_ge(s_sq, m + 1)
                if m == 0:
                    pool.tensor_copy(sq_sum[:, :], sq[:, 0, :]).then_inc(s_sqs, 1)
                else:
                    pool.wait_ge(s_sqs, m)
                    pool.tensor_tensor(sq_sum[:, :], sq_sum[:, :], sq[:, m % 2, :], ALU.add).then_inc(s_sqs, 1)
            with pool.Fori(0, GROUPS) as g:
                for j in range(FG):
                    pool.wait_ge(s_evac, g * GT + (MLP_T0 + j + 1))
                    if j:
                        pool.wait_ge(s_ulo, g * FG + j)
                    pool.tensor_tensor(relu2[:, :], relu[:, j % 2, :], relu[:, j % 2, :], ALU.mult).then_inc(s_relu2, 1)
            pool.wait_ge(s_unit, LAST_UP)
            pool.dma_start(final_w[:, :], io["final_norm_w"].rearrange("(a n) -> a n", a=1)
                           .to_broadcast([P, D])).then_inc(s_fw, 16)
            yp = io["y_prompt"][0].rearrange("(c p) d -> c p d", p=P)
            ys = io["y_sample"].rearrange("b t d -> (b t) d")
            for c in range(NW):
                pool.wait_ge(s_fin_dve, c + 1)
                dst, src = (ys, y[0:NS, 0, :]) if c == 0 else (yp[c - 1], y[:, c, :])
                pool.dma_start(dst, src).then_inc(s_out, 16)
            pool.wait_ge(s_out, 16 * NW)

        def win(ap, c, n=P):
            return ap[:, w0(c):w0(c) + n]

        def halves(ap):
            return ap[:, 0:N].rearrange("p (a n) -> p a n", a=2)

        def prompt(ap):
            return ap[:, T0:N].rearrange("p (c t) -> p c t", c=4)

        def level(ap, b):
            lo = 0 if b < 8 else NS if b == 8 else T0
            return ap[:, lo:N].rearrange("p (n t b) -> p n t b", t=2, b=b)

        def compact(ap, b):
            lo = (0 if b < 8 else NS if b == 8 else T0) // 2
            return ap[:, lo:HALF].rearrange("p (n b) -> p n b", b=b)

        def ctok(c):
            return 0 if c == 0 else (T0 + P * (c - 1)) // 2

        def bank(i, a, n, rows=P):
            return mx[0:rows, i, a:a + n]

        def wins(i, n=NW, w=P):
            return mxf[:, 512 * i:512 * i + n * w].rearrange("p (c t) -> p c t", c=n)

        def sums(i):
            return mx[:, i:i + 2, 0:HALF]

        def pick(ap, h):
            return ap[:, h:h + 1] if isinstance(h, int) else ap[:, bass.ds(h, 1)]

        @block.tensor
        def _(pe):
            mm = pe.matmul

            def ktile(out, ring, k, x_hi, x_lo, kx, first, last_):
                n = 0
                for w, x in ((w_hi, x_hi), (w_hi, x_lo), (w_lo, x_hi)):
                    for half in range(2):
                        ins = mm(out[:, half, :], w[:, ring, k, :], x[:, kx, half * HALF:half * HALF + HALF],
                                 start=first and n == 0, stop=last_ and n == 2)
                    n += 1
                return ins

            def unit(u_, ring, tile, tile_no, kx0, first, last_, x_hi=h_hi, x_lo=h_lo, ready=None, after=None):
                pe.wait_ge(s_lo, u_ + 1)
                if first and not (isinstance(tile_no, int) and tile_no < 2):
                    pe.wait_ge(s_evac, tile_no - 1)
                for k in range(UK):
                    if ready:
                        ready(kx0 + k)
                    ins = ktile(mains(tile), ring, k, x_hi, x_lo, kx0 + k, first and k == 0, last_ and k == UK - 1)
                    if k == UK - 1:
                        ins.then_inc(s_unit, 1)
                    if after:
                        after(k)

            pe.wait_ge(s_small, 16 * 6)
            pe.wait_ge(s_mask, 5)
            n = TAPS * 3 * HEADS
            cpe.done(pe.transpose(bank(0, 0, n), conv_rows[:, :], ident[0:n, 0:n]), "conv_rows")
            n2 = 2 * KT + HEADS + 2
            cpe.done(pe.transpose(bank(1, 0, n2), vec_rows[:, :], ident[0:n2, 0:n2]), "vec_rows")
            cdve.wait(pe, "params", 0)

            def turn_x(k):
                pe.wait_ge(s_x[k // 4], 48)
                if k >= 2:
                    cdve.wait(pe, f"x{k - 2}", 0)
                o = 2 * (k % 2)
                pe.transpose(bank(o, 0, T0), x_tok[0:T0, 0, k * P:k * P + P], ident[0:T0, 0:T0])
                for c in range(1, NW):
                    dst = bank(o, w0(c), P) if c < 4 else bank(o + 1, 0, P)
                    ins = pe.transpose(dst, x_tok[:, c, k * P:k * P + P], ident[:, :])
                cpe.done(ins, f"turn{k}")

            def start_k(k):
                if k % UK == 0:
                    pe.wait_ge(s_lo, k // UK + 1)
                pe.wait_ge(s_k_hi, k + 1)
                pe.wait_ge(s_k_lo, k + 1)
                ins = ktile(mains(0), k // UK, k % UK, h_hi, h_lo, k, k == 0, k == KT - 1)
                if k % UK == UK - 1:
                    ins.then_inc(s_unit, 1)

            for k in range(KT + 2):
                if k < KT:
                    turn_x(k)
                if k >= 2:
                    start_k(k - 2)
            cdve.wait(pe, "diag", 0)
            cdve.wait(pe, "x15", 0)
            mm(bank(0, 0, T0), ones[:, :], diag[:, 0, 0:T0], start=True, stop=True)
            for c in range(1, NW):
                ins = mm(bank(0, w0(c), P) if c < 4 else bank(1, 0, P), ones[:, :], diag[:, c, :], start=True, stop=True)
            cpe.done(ins, "rstd")

            def token_sums(i, src):
                for half in range(2):
                    ins = mm(mx[:, i + half, 0:HALF], ones[:, :], src[:, half * HALF:half * HALF + HALF],
                             start=True, stop=True)
                return ins

            def small_cols():
                cdve.wait(pe, "b", 0)
                cact.wait(pe, "e_exp", 0)
                for c in range(NW):
                    pe.transpose(bank(0, 16 * c, 16), win(b_rows, c), ident[0:16, 0:16])
                for c in range(NW):
                    ins = pe.transpose(bank(1, 16 * c, 16), win(bag2, c), ident[0:16, 0:16])
                cpe.done(ins, "cols")

            def turns(i, src, cs):
                for n_, c in enumerate(cs):
                    ins = pe.transpose(mxf[:, 512 * i + n_ * P:512 * i + n_ * P + P], src(c), ident[:, :])
                return ins

            def t_levels(b):
                return range(NW) if b <= 8 else range(1, NW)

            def gdn(stage, h, first):
                W = lambda steps, name: steps.wait(pe, name, h)
                if stage == "gates":
                    W(gdve, "last")
                    if not first:
                        hdve.wait(pe, "sb", h - 1)
                    for j in range(3):
                        ins = pe.transpose(bank(0, j * P, P, (SB + 1) * PRE), last[:, j, :], ident[:, :])
                    gpe.done(ins, "conv_out")
                elif stage == "norms":
                    W(gact, "square")
                    W(gact, "conv_out")
                    if not first:
                        hact.wait(pe, "oln", h - 1)
                    token_sums(0, rs[:, 0, :])
                    gpe.done(token_sums(2, rs[:, 1, :]), "norms")
                elif stage == "rows":
                    W(gdve, "sel")
                    W(gact, "rln")
                    for i in range(2):
                        for half in range(2):
                            ins = mm(mx[:, 2 * i + half, 0:HALF], ones[0:16, :],
                                     sel[i][:, half * HALF:half * HALF + HALF], start=True, stop=True)
                    gpe.done(ins, "rows")
                elif stage == "scores":
                    W(gdve, "vb")
                    W(gact, "brow")
                    for i, right in ((0, kb), (2, qkv[:, 0, :])):
                        for c in range(NW):
                            ins = mm(mxf[:, 512 * i + c * P:512 * i + c * P + P], win(qkv[:, 1, :], c), win(right, c),
                                     start=True, stop=True)
                    gpe.done(ins, "scores")
                elif stage == "turn_v":
                    W(gdve, "at")
                    gpe.done(turns(0, lambda c: win(vb, c), range(1, NW)), "turn_v")
                elif stage == "turn_k":
                    W(gdve, "qkd")
                    gpe.done(turns(2, lambda c: win(qkv[:, 1, :], c), range(NW)), "turn_k")
                elif stage == "ws0":
                    W(gdve, "keb")
                    pe.wait_ge(s_gst, h * 16 + 16)
                    for b in range(SB):
                        ins = mm(bank(1, ST * b, ST), state[:, b, :], keb[:, ST * b:ST * b + ST], start=True, stop=True)
                    gpe.done(ins, "ws0")
                elif stage == "turn_r0":
                    W(gdve, "r0")
                    gpe.done(pe.transpose(bank(1, P, P), r0T, ident[:, :]), "turn_r0")
                elif stage == "t1":
                    W(gdve, "kd")
                    W(gdve, "tt1")
                    gpe.done(turns(2, lambda c: tT[:, c, :], range(NW)), "t1")
                elif stage[0] == "p" and stage != "p64":
                    b = int(stage[1:])
                    gpool.wait(pe, f"x{b}", h)
                    if b == 2:
                        W(gact, "t1")
                        W(gact, "vt")
                    else:
                        W(gdve, f"t{b // 2}")
                        W(gact, f"p{b // 2}")
                    for c in t_levels(b):
                        left = tm[:, c, :].rearrange("p (n t b) -> p n t b", t=2, b=b)[:, :, 0, :]
                        ins = mm(bank(0, 64 * c, 64), xl[:, c, :], left, start=True, stop=True)
                    gpe.done(ins, stage)
                elif stage[:2] == "tp" and stage != "tp64":
                    b = int(stage[2:])
                    W(gact, f"p{b}")
                    W(gact, "t1" if b == 2 else f"t{b // 2}")
                    W(gact, "r0")
                    for c in t_levels(b):
                        ins = mm(bank(1, 64 * c, 64), tT[:, c, :], pc[:, c, :], start=True, stop=True)
                    gpe.done(ins, stage)
                elif stage[0] == "t" and stage[1:].isdigit():
                    b = int(stage[1:])
                    W(gdve, f"t{b}")
                    if b > 2:
                        W(gact, f"t{b // 2}")
                    gpe.done(turns(2, lambda c: tm[:, c, :], t_levels(b)), stage)
                elif stage == "p64":
                    gpool.wait(pe, "x64", h)
                    W(gdve, "t32")
                    W(gact, "p32")
                    for c in range(1, NW):
                        ins = mm(bank(0, 64 * c, 64), xl[:, c, :], tm[:, c, 0:64], start=True, stop=True)
                    gpe.done(ins, "p64")
                elif stage == "tp64":
                    W(gact, "p64")
                    W(gact, "t32")
                    for c in range(1, NW):
                        ins = mm(bank(1, 64 * c, 64, 64), pc[:, c, :], tT[:, c, 64:P], start=True, stop=True)
                    gpe.done(ins, "tp64")
                elif stage == "vn0":
                    W(gact, "t32")
                    W(gdve, "tt64")
                    gpe.done(mm(bank(1, 384, P), tT[:, 0, :], r, start=True, stop=True), "vn0")
                elif stage == "st0":
                    W(gact, "vn0")
                    for b in range(SB):
                        mm(bank(3, ST * b, ST), state[:, b, :], qe[:, ST * b:ST * b + ST], start=b == 0,
                           stop=False, skip_group_check=True)
                    ins = mm(bank(3, 0, T0), vn, qkd[:, 0, 0:T0], start=False, stop=True, skip_group_check=True)
                    gpe.done(ins, "o0")
                    W(gdve, "vx")
                    for i, n_ in ((0, 4), (1, 4), (2, 1)):
                        ins = mm(bank(i, 0, n_ * P), kdt[:, 0, :], vx[:, 4 * i:4 * i + n_, :], start=True, stop=True)
                    gpe.done(ins, "st0")
                elif stage[:2] == "ws":
                    c = int(stage[3:])
                    W(gdve, f"sc_{c - 1}")
                    gpe.done(mm(bank(0, P * (c - 1), P), win(keb, c), sc[:, (c - 1) % 2, :], start=True, stop=True), stage)
                elif stage[:2] == "vn":
                    c = int(stage[3:])
                    W(gdve, f"r_{c}")
                    gpe.done(mm(bank(1, P * (c - 1), P), tT[:, c, :], r, start=True, stop=True), stage)
                elif stage[:2] == "st":
                    c = int(stage[3:])
                    W(gact, f"vn_{c}")
                    gpe.done(mm(bank(2, P * (c - 1), P), kdt[:, c, :], vn, start=True, stop=True), stage)
                    if c == 1:
                        W(gact, "o0")
                    mm(bank(3, P * (c - 1), P), sc[:, (c - 1) % 2, :], win(qe, c), start=True, stop=False)
                    gpe.done(mm(bank(3, P * (c - 1), P), vn, qkd[:, c, :], start=False, stop=True), f"o_{c}")
                else:
                    assert stage == "out"
                    W(gact, "osq")
                    gpe.done(token_sums(0, rs[:, 0, :]), "out")

            def hg(stage, h, next_first):
                W = lambda steps, name: steps.wait(pe, name, h)
                if stage == "conv_in":
                    if next_first is not None:
                        conv_in(next_first, False)
                elif stage == "gates":
                    pass
                elif stage == "turn_v":
                    gact.wait(pe, "oln", h)
                    hpe.done(turns(0, lambda c: win(hv, c), range(NW)), "turn_v")
                elif stage == "turn_k":
                    W(hdve, "kd")
                    if next_first is not None:
                        gdve.wait(pe, "conv_in", next_first)
                    hpe.done(turns(2, lambda c: win(hkd, c), range(NW)), "turn_k")
                elif stage == "stw":
                    W(hdve, "kdt")
                    W(hdve, "vx")
                    W(hact, "vt")
                    mm(bank(0, 0, P), hkdt[:, 0, :], hvx[:, SB, :], start=True, stop=True)
                    for c in range(1, NW):
                        ins = mm(mxf[:, P * c:P * c + P], hkdt[:, c, :], hvt[:, c, :], start=True, stop=True)
                    hpe.done(ins, "stw")
                elif stage == "diag":
                    for c in range(NW):
                        ins = mm(mxf[:, 1024 + P * c:1024 + P * c + P], win(hk, c), win(hq, c), start=True, stop=True)
                    hpe.done(ins, "diag")
                elif stage[0] == "l":
                    b = int(stage[1:])
                    i = LEVELS.index(b)
                    W(hdve, f"kk{b}")
                    W(hdve, "sc_4" if i < 2 else f"a{LEVELS[i - 2]}")
                    for c in t_levels(b):
                        ins = mm(bank(i % 2, 64 * c, 64), win(hkk, c), hqq[:, ctok(c):ctok(c) + 64], start=True, stop=True)
                    hpe.done(ins, stage)
                elif stage == "o":
                    W(hdve, "a64")
                    W(hact, "eb")
                    pe.wait_ge(s_hst, h * 16 + 16)
                    for b in range(SB):
                        mm(bank(2, ST * b, ST), state[:, b, :], hqe[:, ST * b:ST * b + ST], start=b == 0,
                           stop=False, skip_group_check=True)
                    ins = mm(bank(2, 0, T0), hvt[:, 0, :], ha[:, 0, 0:T0], start=False, stop=True, skip_group_check=True)
                    hpe.done(ins, "o0")
                    for c in range(1, NW):
                        mm(bank(3, P * (c - 1), P), hvt[:, c, :], ha[:, c, :], start=True, stop=False)
                        ins = mm(bank(3, P * (c - 1), P), hsc[:, c - 1, :], win(hqe, c), start=False, stop=True)
                    hpe.done(ins, "o")
                elif stage == "st0":
                    for i in range(2):
                        ins = mm(bank(i, 0, 512), hkdt[:, 0, :], hvx[:, 4 * i:4 * i + 4, :], start=True, stop=True)
                    hpe.done(ins, "st0")
                else:
                    assert stage == "out"
                    W(hact, "osq")
                    hpe.done(token_sums(2, h_arg), "out")

            def conv_in(h, first):
                pe.wait_ge(s_hist, h * 16 + 16)
                if not first:
                    gdve.wait(pe, "sc_4", h - 1)
                for j in range(3):
                    ins = pe.transpose(bank(2, P * j, P), hist_in[:, j, :], ident[:, :])
                gpe.done(ins, "conv_in")

            def mixer_at(stages, run_stage, j):
                def after(k):
                    for st, pos in stages.items():
                        if pos == UK * j + k:
                            run_stage(st)
                return after

            def head(h, first):
                for j in range(16):
                    if j < 8:
                        def run_stage(st):
                            if not first:
                                hg(st, h - 1, h)
                            elif st == "conv_in":
                                conv_in(0, True)
                            elif st == "l1":
                                small_cols()
                        after = mixer_at(HG_STAGES, run_stage, j)
                    else:
                        after = mixer_at(GDN_STAGES, lambda st: gdn(st, h, first), j - 8)
                    unit(h * 16 + (2 + j), j % 2, 1 + j // 2, h * 8 + (1 + j // 2), UK * (j % 2), j % 2 == 0, j % 2 == 1,
                         after=after)

            head(0, True)
            with pe.Fori(1, HEADS) as h:
                head(h, False)
            for st in HG_STAGES:
                hg(st, HEADS - 1, None)

            for i0 in range(1):
                for j in range(4):
                    ready = None
                    if j < 2:
                        def ready(k):
                            pe.wait_ge(s_k_hi, KT + k + 1)
                            pe.wait_ge(s_k_lo, KT + k + 1)
                    unit(OUT_U0 + j, j % 2, 1 + j // 2, OUT_T0 + j // 2, UK * (j % 2), j % 2 == 0, j % 2 == 1, ready=ready)
            with pe.Fori(1, KT // 2) as i:
                for j in range(4):
                    unit(i * 4 + (OUT_U0 + j), j % 2, 1 + j // 2, i * 2 + (OUT_T0 + j // 2), UK * (j % 2), j % 2 == 0,
                         j % 2 == 1)

            def group(g, first):
                for j in range(2 * FG):
                    ready = None
                    if first and j < 2:
                        def ready(k):
                            pe.wait_ge(s_k_hi, 2 * KT + k + 1)
                            pe.wait_ge(s_k_lo, 2 * KT + k + 1)
                    unit(g * GU + (MLP_U0 + j), j % 2, 1 + j // 2, g * GT + (MLP_T0 + j // 2), UK * (j % 2), j % 2 == 0,
                         j % 2 == 1, ready=ready)
                    if first and j == 0:
                        pe.wait_ge(s_sqs, KT)
                        token_sums(0, sq_sum).then_inc(s_n2, 1)
                for m in range(KT):
                    ready = None
                    if m == 0:
                        def ready(k):
                            pe.wait_ge(s_uhi, g * FG + (k + 1))
                            pe.wait_ge(s_ulo, g * FG + (k + 1))
                    unit(g * GU + (MLP_U0 + 2 * FG + m), m % 2, 1 + FG + m, g * GT + (MLP_T0 + FG + m), 0, True, True,
                         x_hi=u_hi, x_lo=u_lo, ready=ready)

            group(0, True)
            with pe.Fori(1, GROUPS) as g:
                group(g, False)
            for m in range(KT):
                if m == 0:
                    pe.wait_ge(s_n2l, 1)
                pe.wait_ge(s_evac, MLP_T0 + GT * (GROUPS - 1) + FG + m + 1)
                if m >= 2:
                    pe.wait_ge(s_fin_copy, m - 1)
                for c in range(NW):
                    o = 1024 * (m % 2) + P * c
                    ins = pe.transpose(mxf[:, o:o + P], win(x1[:, m, :], c), ident[:, :])
                ins.then_inc(s_fin_pe, 1)

        @block.scalar
        def _(act):
            A = act.activation

            def hi(u_, ring):
                if isinstance(u_, int):
                    act.wait_ge(s_w[ring], 16 * (u_ // RAW + 1))
                    if u_ >= 2:
                        act.wait_ge(s_unit, u_ - 1)
                    A(w_hi[:, ring % 2], w_raw[:, ring], ACT.Copy).then_inc(s_hi, 1)
                else:
                    loop, per, base = u_
                    act.wait_ge(s_w[ring], loop * (16 * per // RAW) + 16 * (base // RAW + 1))
                    act.wait_ge(s_unit, loop * per + (base - 1))
                    A(w_hi[:, ring % 2], w_raw[:, ring], ACT.Copy).then_inc(s_hi, 1)

            def hi_at(loop, per, base):
                hi(loop * per + base if isinstance(loop, int) else (loop, per, base), base % RAW)

            act.preload_act_table_set("natural_log_exp_and_others")
            act.wait_ge(s_mask, 5)
            hi(0, 0)
            hi(1, 1)
            cdve.wait(act, "params", 0)
            for q in range(4):
                act.wait_ge(s_x[q], 48)
                for k in range(4 * q, 4 * q + 4):
                    cdve.wait(act, f"x{k}", 0)
                    A(h_hi[:, k, :], xT[:, k, :], ACT.Copy, scale=vecs[:, k:k + 1]).then_inc(s_k_hi, 1)
                cdve.wait(act, "ssq0", 0)
                for c in range(NW):
                    rows = T0 if c == 0 else P
                    if NW * q + c:
                        act.wait_ge(s_dump, NW * q + c)
                    A(sq_dump[0:rows, :], x_tok[0:rows, c, 512 * q:512 * q + 512], ACT.Square,
                      accum_out=ssq[0:rows, c, q:q + 1]).then_inc(s_dump, 1)
            hi(2, 2)
            cdve.wait(act, "ssum", 0)
            cact.done(A(ssum[:, :], ssum[:, :], ACT.Ln, bias=eps[:, :], scale=1.0 / D), "ln")
            cact.wait(act, "ln", 0)
            cact.done(A(ssum[:, :], ssum[:, :], ACT.Exp, scale=-0.5), "exp")

            def small():
                act.wait_ge(s_small, 16 * 8)
                act.wait_ge(s_mask, MASK_STEPS)
                cact.done(A(a_exp[:, :], a_exp[:, :], ACT.Exp), "a")
                cdve.wait(act, "lb0", 0)
                cact.done(A(lb_tmp[:, 1, :], lb_tmp[:, 0, :], ACT.Exp), "lb")
                cdve.wait(act, "dt", 0)
                cact.done(A(bag1, bag, ACT.Exp, scale=-1.0), "b_exp")
                cdve.wait(act, "clamp", 0)
                cact.done(A(bag1, bag1, ACT.Ln, bias=1.0), "b_ln")
                cact.wait(act, "b_ln", 0)
                cact.done(A(beta_rows[:, :], bag1, ACT.Exp, scale=-1.0), "b_sig")
                cdve.wait(act, "abs", 0)
                cact.done(A(bag2, bag2, ACT.Exp, scale=-1.0), "s_exp")
                cact.wait(act, "s_exp", 0)
                cact.done(A(bag2, bag2, ACT.Ln, bias=1.0), "s_ln")
                cdve.wait(act, "e_arg", 0)
                cact.done(A(bag2, bag2, ACT.Exp), "e_exp")

            def gdn(stage, h, first):
                W = lambda steps, name: steps.wait(act, name, h)
                done = gact.done
                if stage == "gates":
                    W(gpe, "conv_out")
                    if not first:
                        act.wait_ge(s_hist_out, h * 32)
                    done(A(hist_out[:, :, :], wins(0, 3)[0:(SB + 1) * PRE], ACT.Copy), "conv_out")
                    W(gdve, "conv_2")
                    if not first:
                        hdve.wait(act, "y", h - 1)
                        act.wait_ge(s_hmix, h * 16)
                        act.wait_ge(s_hsc_out, h * 16)
                    done(A(gate, conv, ACT.Exp, scale=-1.0), "exp")
                    W(gdve, "clamp")
                    done(A(gate, gate, ACT.Ln, bias=1.0), "ln")
                    W(gact, "ln")
                    done(A(gate, gate, ACT.Exp, scale=-1.0), "sig")
                    act.wait_ge(s_evac, h * 8 + 5)
                    done(A(gze, gz[:, :], ACT.Exp, scale=-1.0), "zexp")
                    W(gdve, "zclamp")
                    done(A(gze, gze, ACT.Ln, bias=1.0), "zln")
                    W(gact, "zln")
                    done(A(gze, gze, ACT.Exp, scale=-1.0), "zsig")
                    W(gdve, "qkv")
                    done(A(rs, qkv[:, 0:2, :], ACT.Square), "square")
                elif stage == "norms":
                    W(gpe, "norms")
                    done(A(rs.rearrange("p a (b n) -> p (a b) n", b=2), mx[:, :, 0:HALF], ACT.Ln, bias=eps[:, :]), "rln")
                    W(gact, "rln")
                    done(A(rs, rs, ACT.Exp, scale=-0.5), "rexp")
                elif stage == "rows":
                    W(gpe, "rows")
                    done(A(halves(b_row), sums(2), ACT.Copy), "brow")
                    W(gact, "brow")
                    done(A(eb, b_row, ACT.Exp), "eb")
                    W(gdve, "diff")
                    done(A(decay, decay, ACT.Exp), "decay")
                elif stage == "turn_v":
                    W(gpe, "turn_v")
                    done(A(vbt, wins(0, 4), ACT.Copy), "vt")
                elif stage == "turn_r0":
                    W(gpe, "turn_r0")
                    done(A(r, bank(1, P, P), ACT.Copy), "r0")
                elif stage == "t1":
                    W(gpe, "t1")
                    done(A(tm, wins(2), ACT.Copy), "t1")
                elif stage[0] == "p":
                    W(gpe, stage)
                    b = int(stage[1:])
                    c0 = 0 if b <= 8 else 1
                    done(A(pc[:, c0:, :], wins(0, NW, 64)[:, c0:, :], ACT.Copy), stage)
                elif stage[0] == "t" and stage[1:].isdigit():
                    W(gpe, stage)
                    c0 = 0 if int(stage[1:]) <= 8 else 1
                    done(A(tT[:, c0:, :], wins(2, NW - c0), ACT.Copy), stage)
                elif stage == "vn0":
                    W(gpe, "vn0")
                    done(A(vn, bank(1, 384, P), ACT.Copy), "vn0")
                elif stage == "st0":
                    W(gpe, "o0")
                    done(A(go[:, 0:T0], bank(3, 0, T0), ACT.Copy), "o0")
                elif stage[:2] == "vn":
                    c = int(stage[3:])
                    W(gpe, stage)
                    done(A(vn, bank(1, P * (c - 1), P), ACT.Copy), stage)
                elif stage[:2] == "st":
                    c = int(stage[3:])
                    W(gpe, f"o_{c}")
                    done(A(win(go, c), bank(3, P * (c - 1), P), ACT.Copy), f"o_{c}")
                    if c == NW - 1:
                        W(gact, f"o_{c}")
                        done(A(rs[:, 0, :], go, ACT.Square), "osq")
                elif stage == "out":
                    W(gpe, "out")
                    done(A(halves(rs[:, 1, :]), sums(0), ACT.Ln, bias=eps[:, :], scale=1.0 / P), "oln")
                    W(gact, "oln")
                    done(A(rs[:, 1, :], rs[:, 1, :], ACT.Exp, scale=-0.5), "oexp")

            def hg(stage, h):
                W = lambda steps, name: steps.wait(act, name, h)
                done = hact.done
                if stage == "gates":
                    act.wait_ge(s_evac, h * 8 + 9)
                    done(A(hf[:, :], hf[:, :], ACT.Exp, scale=-1.0), "exp")
                    gdve.wait(act, "y", h)
                    act.wait_ge(s_gmix, h * 16 + 16)
                    act.wait_ge(s_gsc_out, h * 16 + 16)
                    done(A(ho, hz[:, :], ACT.Exp, scale=-1.0), "zexp")
                    W(hdve, "clamp")
                    done(A(hl, hf[:, :], ACT.Ln, bias=1.0), "ln")
                    done(A(hkd, hf[:, :], ACT.Ln, bias=1.0, scale=pick(lb, h)), "lnlb")
                    W(hact, "ln")
                    done(A(heb, hl, ACT.Exp, scale=-1.0), "sig")
                    W(hdve, "zclamp")
                    done(A(ho, ho, ACT.Ln, bias=1.0), "zln")
                    W(hact, "zln")
                    done(A(ho, ho, ACT.Exp, scale=-1.0), "zsig")
                    W(hdve, "b")
                    W(hdve, "k")
                    done(A(heb, hb, ACT.Exp), "eb")
                    W(hdve, "kdarg")
                    done(A(hkd, hkd, ACT.Exp), "kdexp")
                elif stage == "turn_v":
                    W(hpe, "turn_v")
                    done(A(hvt, wins(0), ACT.Copy), "vt")
                elif stage[0] == "l":
                    b = int(stage[1:])
                    W(hdve, f"arg{b}")
                    v = h_arg[:, (0 if b < 8 else NS if b == 8 else T0):N]
                    done(A(v, v, ACT.Exp), f"e{b}")
                elif stage == "o":
                    W(hpe, "o0")
                    done(A(ho[:, 0:T0], bank(2, 0, T0), ACT.Copy), "o0")
                    W(hpe, "o")
                    done(A(prompt(ho), wins(3, 4), ACT.Copy), "o")
                    W(hact, "o")
                    done(A(h_arg, ho, ACT.Square), "osq")
                elif stage == "out":
                    W(hpe, "out")
                    done(A(halves(hl), sums(2), ACT.Ln, bias=eps[:, :], scale=1.0 / P), "oln")
                    W(hact, "oln")
                    done(A(hl, hl, ACT.Exp, scale=-0.5), "oexp")

            def head(h, first):
                for j in range(16):
                    hi_at(h, 16, 3 + j)
                    if j < 8:
                        for st, pos in HG_STAGES.items():
                            if pos // UK == j and not first:
                                hg(st, h - 1)
                        if first and j == 1:
                            small()
                    else:
                        for st, pos in GDN_STAGES.items():
                            if pos // UK == j - 8:
                                gdn(st, h, first)

            head(0, True)
            with act.Fori(1, HEADS) as h:
                head(h, False)
            for st in HG_STAGES:
                hg(st, HEADS - 1)

            hi(OUT_U0 + 1, (OUT_U0 + 1) % RAW)
            for k in range(KT):
                act.wait_ge(s_mixin[k % 4], 16 * (k // 4 + 1))
                act.wait_ge(s_unit, OUT_U0)
                A(h_hi[:, k, :], mix_in[:, k % 4, :], ACT.Copy).then_inc(s_k_hi, 1)

            def square(m, slot):
                act.wait_ge(s_evac, m + (OUT_T0 + 1))
                if not isinstance(m, int) or m >= 2:
                    act.wait_ge(s_sqs, m - 1)
                A(sq[:, slot, :], x1[:, m, :] if isinstance(m, int) else x1[:, bass.ds(m, 1), :].rearrange(
                    "p a n -> p (a n)"), ACT.Square).then_inc(s_sq, 1)

            for j in range(4):
                hi_at(0, 4, OUT_U0 + j + 1) if j else None
                if j == 2:
                    square(0, 0)
            for i in range(1, KT // 2):
                for j in range(4):
                    hi_at(i, 4, OUT_U0 + j + 1)
                    if j == 0:
                        square(2 * i - 1, 1)
                    if j == 2:
                        square(2 * i, 0)
            hi(MLP_U0 + 1, (MLP_U0 + 1) % RAW)
            square(KT - 1, 1)
            for k in range(KT):
                act.wait_ge(s_unit, MLP_U0)
                act.wait_ge(s_evac, OUT_T0 + k + 1)
                A(h_hi[:, k, :], x1[:, k, :], ACT.Copy, scale=norm2_w[:, k:k + 1]).then_inc(s_k_hi, 1)
            act.wait_ge(s_n2, 1)
            A(halves(rstd[:, :]), sums(0), ACT.Ln, bias=eps[:, :], scale=1.0 / D).then_inc(s_n2l, 1)
            act.wait_ge(s_n2l, 1)
            A(rstd[:, :], rstd[:, :], ACT.Exp, scale=-0.5).then_inc(s_n2l, 1)

            def up_square(g, j):
                act.wait_ge(s_evac, g * GT + (MLP_T0 + j + 1))
                A(u_hi[:, j, :], relu[:, j % 2, :], ACT.Square).then_inc(s_uhi, 1)

            def group(g, first, last_):
                for j in range(GU):
                    if not (first and j == 0) and not (last_ and j == GU - 1):
                        hi_at(g, GU, MLP_U0 + j + 1)
                    if j % 2 == 0 and 2 <= j <= 2 * FG:
                        up_square(g, j // 2 - 1)

            group(0, True, False)
            with act.Fori(1, GROUPS - 1) as g:
                group(g, False, False)
            group(GROUPS - 1, False, True)

            for m in range(0, KT, 2):
                act.wait_ge(s_unit, LAST_UP)
                act.wait_ge(s_fin_pe, m + 1)
                if m:
                    act.wait_ge(s_fin_copy, m)
                A(y[:, :, m * P:m * P + P], wins(0), ACT.Copy).then_inc(s_fin_copy, 1)
            act.wait_ge(s_fin_copy, KT)
            for c in range(NW):
                act.wait_ge(s_fin_pe, KT)
                if c:
                    act.wait_ge(s_fin, 3 * c)
                A(mxf[:, :], y[:, c, :], ACT.Square, accum_out=fin[:, c:c + 1]).then_inc(s_fin, 1)
                act.wait_ge(s_fin, 3 * c + 1)
                A(fin[:, c:c + 1], fin[:, c:c + 1], ACT.Ln, bias=eps[:, :], scale=1.0 / D).then_inc(s_fin, 1)
                act.wait_ge(s_fin, 3 * c + 2)
                A(fin[:, c:c + 1], fin[:, c:c + 1], ACT.Exp, scale=-0.5).then_inc(s_fin, 1)

        @block.vector
        def _(dve):
            dve.memset(dve_spare[:, :], 0.0)
            TT, TS, STT = dve.tensor_tensor, dve.tensor_scalar, dve.scalar_tensor_tensor

            def lo(u_, ring, base=None):
                dve.wait_ge(s_hi, u_ + 1)
                TT(w_lo[:, ring % 2], w_raw[:, ring], w_hi[:, ring % 2].bitcast(F32), ALU.subtract).then_inc(s_lo, 1)

            def k_lo(src, k, n_, scale=None):
                dve.wait_ge(s_k_hi, n_ + 1)
                if scale is None:
                    TT(h_lo[:, k, :], src, h_hi[:, k, :].bitcast(F32), ALU.subtract).then_inc(s_k_lo, 1)
                else:
                    STT(h_lo[:, k, :], src, scale, h_hi[:, k, :].bitcast(F32), ALU.mult, ALU.subtract).then_inc(s_k_lo, 1)

            def scan(out, g, rows=P):
                return dve.tensor_tensor_scan(out, run[0:rows, :], g, 0.0, ALU.mult, ALU.add)

            lo(0, 0)
            lo(1, 1)
            cpe.wait(dve, "vec_rows", 0)
            dve.tensor_copy(conv_w[:, :, :, :].rearrange("p w j h -> p (w j h)"), bank(0, 0, TAPS * 3 * HEADS))
            cdve.done(dve.tensor_copy(vecs[:, :], bank(1, 0, 2 * KT + HEADS + 2)), "params")
            cdve.done(dve.memset(ssq[:, :, :], 1.0), "ssq0")
            for k in range(KT):
                cpe.wait(dve, f"turn{k}", 0)
                o = 2 * (k % 2)
                dve.tensor_copy(xT[:, k, 0:w0(4)], bank(o, 0, w0(4)))
                cdve.done(dve.tensor_copy(xT[:, k, w0(4):N], bank(o + 1, 0, P)), f"x{k}")
                k_lo(xT[:, k, :], k, k, vecs[:, k:k + 1])
            dve.wait_ge(s_dump, 4 * NW)
            cdve.done(dve.tensor_reduce(ssum[:, :], ssq[:, :, :], AX.X, ALU.add), "ssum")
            dve.wait_ge(s_unit, 1)
            lo(2, 2)
            cact.wait(dve, "exp", 0)
            cdve.done(TT(diag[:, :, :], ident[:, :].unsqueeze(1).to_broadcast([P, NW, P]),
                         ssum[:, :].unsqueeze(2).to_broadcast([P, NW, P]), ALU.mult), "diag")
            cpe.wait(dve, "rstd", 0)
            dve.tensor_copy(rstd[:, 0:w0(4)], bank(0, 0, w0(4)))
            cdve.done(dve.tensor_copy(rstd[:, w0(4):N], bank(1, 0, P)), "rstd")

            def end_arg(out, b, rows=P):
                for o, v in ((seq(out), seq(b)), (out[:, NS:T0].unsqueeze(1), b[:, NS:T0].unsqueeze(1)),
                             (prompt(out), prompt(b))):
                    n_, t = v.shape[1], v.shape[2]
                    ins = TT(o, v[:, :, t - 1:t].to_broadcast([rows, n_, t]), v, ALU.subtract)
                return ins

            def small_start():
                dve.wait_ge(s_mask, MASK_STEPS)
                cdve.done(TT(lb_tmp[:, 0, :], lb_raw, lb_raw, ALU.subtract), "lb0")
                cact.wait(dve, "lb", 0)
                cdve.done(dve.reciprocal(lb_tmp[:, 0, :], lb_tmp[:, 1, :]), "lb1")
                cdve.wait(dve, "lb1", 0)
                cdve.done(TT(lb_tmp[:, 1, :], lb_tmp[:, 1, :], lb_tmp[:, 0, :], ALU.mult), "lb2")
                cdve.wait(dve, "lb2", 0)
                cdve.done(TT(lb[:, :], lb_tmp[:, 1, :], lb_tmp[:, 1, :], ALU.subtract), "lb3")
                cdve.wait(dve, "lb3", 0)
                cdve.done(TS(one_lb[:, :], lb[:, :], -1.0, 1.0, ALU.mult, ALU.add), "one_lb")
                dve.wait_ge(s_unit, 2)
                cdve.wait(dve, "rstd", 0)
                TT(halves(bag), mains(0)[0:16], halves(rstd[0:16, :]), ALU.mult).then_inc(s_evac, 1)
                dve.wait_ge(s_small, 16 * 8)
                dve.wait_ge(s_evac, 1)
                cdve.done(TS(bag, bag, dt_bias[:, 0:1], None, ALU.add), "dt")

            def small_rest():
                cact.wait(dve, "b_exp", 0)
                cdve.done(TS(bag1, bag1, BIG, None, ALU.min), "clamp")
                cdve.done(STT(bag2, bag, -1.0, bag, ALU.mult, ALU.max), "abs")
                cact.wait(dve, "s_ln", 0)
                cdve.done(STT(bag, bag, 0.0, bag2, ALU.max, ALU.add), "soft")
                cdve.wait(dve, "soft", 0)
                cdve.done(TS(bag, bag, a_exp[:, 0:1], -1.0, ALU.mult, ALU.mult), "g")
                cdve.wait(dve, "g", 0)
                cdve.done(scan(b_rows[:, :], bag, 16), "b")
                cdve.wait(dve, "b", 0)
                cdve.done(end_arg(bag2, b_rows, 16), "e_arg")

            def small_end():
                cpe.wait(dve, "cols", 0)
                dve.tensor_copy(b_col[:, :, :], bank(0, 0, 16 * NW).rearrange("p (c n) -> p c n", c=NW))
                cdve.done(dve.tensor_copy(e_col[:, :, :], bank(1, 0, 16 * NW).rearrange("p (c n) -> p c n", c=NW)), "cols")

            def evacuate(tile, j, h):
                p = mains(tile)
                if j >= 3:
                    dst = {3: gz, 4: hq, 5: hf, 6: hv, 7: hz}[j]
                    TT(halves(dst[:, :]), p, halves(rstd[:, :]), ALU.mult).then_inc(s_evac, 1)
                    return
                n1 = HALF - NS
                TT(u[:, j, 0:UP0].rearrange("p (b t) -> p b t", b=SB)[:, :, PRE:USEQ], seq(p[:, 0, :]), seq(rstd),
                   ALU.mult)
                TT(u[:, j, UP0 + PRE:UP0 + PRE + n1], p[:, 0, NS:HALF], rstd[:, NS:HALF], ALU.mult)
                TT(u[:, j, UP0 + PRE + n1:UW], p[:, 1, :], rstd[:, HALF:N], ALU.mult).then_inc(s_evac, 1)

            def convolve(j, h):
                o = conv[:, j, :]
                for t in range(TAPS):
                    if isinstance(h, int):
                        w = conv_w[:, t, j, h:h + 1]
                    else:
                        w = conv_w[:, t, j, bass.ds(h, 1)]
                    x = u[:, j, t:t + CW]
                    if t == 0:
                        dve.wait_ge(s_evac, h * 8 + (2 + j))
                        gdve.wait(dve, "conv_in", h)
                        ins = TS(o, x, w, None, ALU.mult)
                        ins.then_inc(s_tap, 1)
                    else:
                        dve.wait_ge(s_tap, h * 9 + (3 * j + t))
                        ins = STT(o, x, w, o, ALU.mult, ALU.add)
                        if t < TAPS - 1:
                            ins.then_inc(s_tap, 1)
                gdve.done(ins, f"conv_{j}")

            def gdn(stage, h, first):
                W = lambda steps, name: steps.wait(dve, name, h)
                done = gdve.done
                if stage == "gates":
                    if not first:
                        dve.wait_ge(s_hmix, h * 16)
                        dve.wait_ge(s_hsc_out, h * 16)
                    TS(sel[0], beta_rows[:, :], pick(one_hot, h), None, ALU.mult)
                    done(TS(sel[1], b_rows[:, :], pick(one_hot, h + HEADS), None, ALU.mult), "sel")
                    W(gact, "exp")
                    done(TS(gate, gate, BIG, None, ALU.min), "clamp")
                    W(gact, "zexp")
                    done(TS(gze, gze, BIG, None, ALU.min), "zclamp")
                    W(gact, "sig")
                    s_in = lambda a, j: a[:, j, 0:UP0].rearrange("p (b t) -> p b t", b=SB)[:, :, 0:ST]
                    for j in range(3):
                        TT(seq(qkv[:, j, :]), s_in(conv, j), s_in(gate, j), ALU.mult)
                    done(TT(qkv[:, :, NS:N], conv[:, :, UP0:CW], gate[:, :, UP0:CW], ALU.mult), "qkv")
                    W(gact, "zsig")
                    done(TT(gz[:, :], gz[:, :], gze, ALU.mult), "zs")
                elif stage == "norms":
                    W(gact, "rexp")
                    done(STT(qkv[:, 0, :], qkv[:, 0, :], float(P) ** -0.5, rs[:, 0, :], ALU.mult, ALU.mult), "qn")
                    done(TT(qkv[:, 1, :], qkv[:, 1, :], rs[:, 1, :], ALU.mult), "kn")
                elif stage == "rows":
                    W(gpe, "rows")
                    W(gdve, "kn")
                    done(TT(halves(kb), halves(qkv[:, 1, :]), sums(0), ALU.mult), "kb")
                    done(TT(halves(vb), halves(qkv[:, 2, :]), sums(0), ALU.mult), "vb")
                    W(gact, "brow")
                    for c in range(NW):
                        ins = TS(decay[:, c, :], win(b_row, c), pick(b_col[:, c, :], h + HEADS), 0.0,
                                 ALU.subtract, ALU.min)
                    done(ins, "diff")
                    W(gact, "eb")
                    W(gdve, "kb")
                    done(TT(keb, kb, eb, ALU.mult), "keb")
                    done(TT(qe, qkv[:, 0, :], eb, ALU.mult), "qe")
                    W(gact, "decay")
                    done(TT(decay, decay, causal[:, :, :], ALU.mult), "dm")
                elif stage == "scores":
                    W(gpe, "scores")
                    W(gdve, "dm")
                    done(TT(aT, wins(0), decay, ALU.mult), "at")
                    done(TT(qkd, wins(2), decay, ALU.mult), "qkd")
                    W(gdve, "at")
                    done(TT(tT, aT, masks[:, 0:1, :].to_broadcast([P, NW, P]), ALU.mult), "tt0")
                    W(gdve, "tt0")
                    done(TT(tT, ident[:, :].unsqueeze(1).to_broadcast([P, NW, P]), tT, ALU.subtract), "tt1")
                elif stage == "turn_k":
                    W(gpe, "turn_k")
                    e = e_col[:, :, h + HEADS:h + HEADS + 1] if isinstance(h, int) else e_col[:, :, bass.ds(h + HEADS, 1)]
                    done(TT(kdt, wins(2), e.to_broadcast([P, NW, P]), ALU.mult), "kd")
                elif stage == "ws0":
                    W(gpe, "ws0")
                    TT(r0T[:, 0:NS], vb[:, 0:NS], bank(1, 0, NS), ALU.subtract)
                    done(dve.tensor_copy(r0T[:, NS:P], vb[:, NS:P]), "r0")
                elif stage[:2] == "tp" and stage != "tp64":
                    b = int(stage[2:])
                    W(gpe, stage)
                    c0 = 0 if b <= 8 else 1
                    left = tm[:, c0:, :].rearrange("p c (n t b) -> p (c n) t b", t=2, b=b)[:, :, 0, :]
                    part = wins(1, NW, 64)[:, c0:, :].rearrange("p c (n b) -> p (c n) b", b=b)
                    done(TT(left, left, part, ALU.subtract), f"t{b}")
                elif stage == "tp64":
                    W(gpe, "tp64")
                    o = tT[0:64, 1:, 64:P]
                    done(TT(o, o, wins(1, NW, 64)[0:64, 1:, :], ALU.subtract), "tt64")
                elif stage == "vn0":
                    W(gact, "vn0")
                    W(gpe, "scores")
                    done(TT(vx, vn.unsqueeze(1).to_broadcast([P, SB + 1, P]),
                            seq_rows[:, :].unsqueeze(2).to_broadcast([P, SB + 1, P]), ALU.mult), "vx")
                elif stage == "st0":
                    W(gpe, "o0")
                    last_ = seq(eb)[:, :, ST - 1:ST].to_broadcast([P, SB, P])
                    done(TT(state[:, :, :], state[:, :, :], last_, ALU.mult), "sb_scale")
                    W(gpe, "st0")
                    W(gdve, "sb_scale")
                    done(TT(state[:, :, :], state[:, :, :], wins(0, SB), ALU.add), "sb")
                    if not first:
                        dve.wait_ge(s_gsc_out, h * 16)
                    done(dve.tensor_copy(sc[:, 0, :], bank(2, 0, P)), "sc_0")
                elif stage[:2] == "ws":
                    c = int(stage[3:])
                    W(gpe, stage)
                    done(TT(r, vbt[:, c - 1, :], bank(0, P * (c - 1), P), ALU.subtract), f"r_{c}")
                elif stage[:2] == "st":
                    c = int(stage[3:])
                    W(gpe, f"o_{c}")
                    W(gdve, f"sc_{c - 1}")
                    end = w0(c) + P - 1
                    done(STT(sc[:, c % 2, :], sc[:, (c - 1) % 2, :], eb[:, end:end + 1], bank(2, P * (c - 1), P),
                             ALU.mult, ALU.add), f"sc_{c}")
                elif stage == "out":
                    W(gact, "oexp")
                    done(STT(go, go, gdn_w, rs[:, 1, :], ALU.mult, ALU.mult), "y1")
                    W(gdve, "y1")
                    W(gdve, "zs")
                    done(TT(go, go, gz[:, :], ALU.mult), "y")

            def take_level(i, h):
                b = LEVELS[i]
                W = lambda steps, name: steps.wait(dve, name, h)
                W(hpe, f"l{b}")
                W(hdve, f"a{LEVELS[i - 1]}" if i else "diag")
                settle(dve, dve_spare, dset, f"l{b}", h)
                c0 = 0 if b < 8 else 1
                if b == 8:
                    m0 = NS // 2
                    dve.copy_predicated(ha[NS:T0, 0, NS + 8:T0], pmask[NS:T0, i, m0:m0 + 8],
                                        mx[NS:T0, i % 2, m0:m0 + 8])
                right = ha[:, c0:, :].rearrange("p c (n t b) -> p (c n) t b", t=2, b=b)[:, :, 1, :]
                msk = pmask[:, i, 64 * c0:NW * 64].rearrange("p (n b) -> p n b", b=b)
                dat = mx[:, i % 2, 64 * c0:NW * 64].rearrange("p (n b) -> p n b", b=b)
                hdve.done(dve.copy_predicated(right, msk, dat), f"a{b}")

            def hg(stage, h, nxt):
                W = lambda steps, name: steps.wait(dve, name, h)
                done = hdve.done
                if stage == "conv_in":
                    if nxt is not None:
                        history(nxt)
                elif stage == "gates":
                    W(hact, "exp")
                    done(TS(hf[:, :], hf[:, :], BIG, None, ALU.min), "clamp")
                    W(hact, "zexp")
                    done(TS(ho, ho, BIG, None, ALU.min), "zclamp")
                    W(hact, "lnlb")
                    W(hact, "sig")
                    done(TT(hl, hkd, hl, ALU.subtract), "g")
                    done(TS(hk, hf[:, :], pick(one_lb, h), None, ALU.mult), "k0")
                    W(hdve, "k0")
                    done(TT(hk, hk, heb, ALU.mult), "k")
                    W(hdve, "g")
                    done(scan(hb, hl), "b")
                    W(hact, "zsig")
                    done(TT(hz[:, :], hz[:, :], ho, ALU.mult), "zs")
                    W(hdve, "b")
                    done(end_arg(hkd, hb), "kdarg")
                    W(hact, "eb")
                    done(TT(hqe, hq[:, :], heb, ALU.mult), "qe")
                    W(hact, "kdexp")
                    W(hdve, "k")
                    done(TT(hkd, hkd, hk, ALU.mult), "kd")
                elif stage == "turn_v":
                    W(hact, "vt")
                    done(TT(hvx, hvt[:, 0:1, :].to_broadcast([P, SB + 1, P]),
                            seq_rows[:, :].unsqueeze(2).to_broadcast([P, SB + 1, P]), ALU.mult), "vx")
                elif stage == "turn_k":
                    W(hpe, "turn_k")
                    done(dve.tensor_copy(hkdt, wins(2)), "kdt")
                elif stage == "stw":
                    W(hpe, "stw")
                    done(dve.tensor_copy(hsc[:, 0, :], bank(0, 0, P)), "sc_0")
                    for c in range(1, NW):
                        W(hdve, f"sc_{c - 1}")
                        end = w0(c) + P - 1
                        done(STT(hsc[:, c, :], hsc[:, c - 1, :], heb[:, end:end + 1], mxf[:, P * c:P * c + P],
                                 ALU.mult, ALU.add), f"sc_{c}")
                elif stage == "diag":
                    W(hpe, "diag")
                    hpool.wait(dve, "zero", h)
                    settle(dve, dve_spare, dset, "diag", h)
                    done(dve.copy_predicated(ha, imask[:, :, :], wins(2)), "diag")
                elif stage[0] == "l":
                    b = int(stage[1:])
                    i = LEVELS.index(b)
                    if i:
                        W(hdve, f"kk{LEVELS[i - 1]}")
                    v, o = level(hb, b), level(h_arg, b)
                    ref = v[:, :, 0, b - 1:b].to_broadcast([P, v.shape[1], b])
                    TT(o[:, :, 0, :], ref, v[:, :, 0, :], ALU.subtract)
                    done(TT(o[:, :, 1, :], v[:, :, 1, :], ref, ALU.subtract), f"arg{b}")
                    if i:
                        take_level(i - 1, h)
                    W(hact, f"e{b}")
                    if i:
                        W(hpe, f"l{LEVELS[i - 1]}")
                    done(TT(compact(hqq, b), level(hq, b)[:, :, 1, :], o[:, :, 1, :], ALU.mult), f"q{b}")
                    done(TT(level(hkk, b)[:, :, 0, :], level(hk, b)[:, :, 0, :], o[:, :, 0, :], ALU.mult), f"kk{b}")
                    if b == LEVELS[-1]:
                        take_level(i, h)
                elif stage == "st0":
                    W(hpe, "o")
                    last_ = seq(heb)[:, :, ST - 1:ST]
                    done(TT(state[:, :, :], state[:, :, :], last_.to_broadcast([P, SB, P]), ALU.mult), "sb_scale")
                    W(hpe, "st0")
                    W(hdve, "sb_scale")
                    done(TT(state[:, :, :], state[:, :, :], wins(0, SB), ALU.add), "sb")
                elif stage == "out":
                    W(hact, "oexp")
                    done(STT(ho, ho, hg_w, hl, ALU.mult, ALU.mult), "y1")
                    W(hdve, "y1")
                    W(hdve, "zs")
                    done(TT(ho, ho, hz[:, :], ALU.mult), "y")

            def history(h):
                gpe.wait(dve, "conv_in", h)
                for j in range(3):
                    ins = dve.tensor_copy(u[:, j, 0:UP0].rearrange("p (b t) -> p b t", b=SB)[:, :, 0:PRE],
                                          bank(2, j * P, SB * PRE).rearrange("p (b t) -> p b t", b=SB))
                gdve.done(ins, "conv_in")

            def save_last(h):
                dve.wait_ge(s_evac, h * 8 + 4)
                n_ = SB * PRE
                for j in range(3):
                    dve.tensor_copy(last[:, j, 0:n_].rearrange("p (b t) -> p b t", b=SB),
                                    u[:, j, 0:UP0].rearrange("p (b t) -> p b t", b=SB)[:, :, ST:USEQ])
                gdve.done(dve.tensor_copy(last[:, :, n_:n_ + PRE], u[:, :, UW - PRE:UW]), "last")

            def head(h, first):
                for j in range(16):
                    if j % 2 == 0 and not (first and j == 0):
                        dve.wait_ge(s_unit, h * 16 + (2 + j))
                        evacuate(j // 2, (j // 2 - 1) % 8, h)
                    if first and j == 0:
                        dve.wait_ge(s_mask, MASK_STEPS)
                    lo(h * 16 + (3 + j), (3 + j) % RAW)
                    if j < 8:
                        for st, pos in HG_STAGES.items():
                            if pos // UK == j:
                                if not first:
                                    hg(st, h - 1, h)
                                elif st == "conv_in":
                                    history(0)
                        if first:
                            if j == 0:
                                small_start()
                            if j == 1:
                                small_rest()
                            if j == 4:
                                small_end()
                        if j in (2, 4, 6):
                            convolve(j // 2 - 1, h)
                        if j == 6:
                            save_last(h)
                    else:
                        for st, pos in GDN_STAGES.items():
                            if pos // UK == j - 8:
                                gdn(st, h, first)

            head(0, True)
            with dve.Fori(1, HEADS) as h:
                head(h, False)
            dve.wait_ge(s_unit, OUT_U0)
            evacuate(0, 7, HEADS - 1)
            for st in HG_STAGES:
                hg(st, HEADS - 1, None)
            lo(OUT_U0 + 1, (OUT_U0 + 1) % RAW)
            for k in range(KT):
                k_lo(mix_in[:, k % 4, :], k, KT + k)

            def residual(t, m):
                o = halves(x1[:, m, :])
                TT(o, o, mains(t), ALU.add).then_inc(s_evac, 1)

            for i in range(KT // 2):
                for j in range(4):
                    if j == 0 and i:
                        dve.wait_ge(s_unit, OUT_U0 + 4 * i)
                        residual(OUT_T0 + 2 * i - 1, 2 * i - 1)
                    if j == 2:
                        dve.wait_ge(s_unit, OUT_U0 + 4 * i + 2)
                        if i == 0:
                            dve.wait_ge(s_xT, 16)
                        residual(OUT_T0 + 2 * i, 2 * i)
                    if i or j:
                        lo(OUT_U0 + 4 * i + j + 1, (OUT_U0 + j + 1) % RAW)
            dve.wait_ge(s_unit, MLP_U0)
            residual(OUT_T0 + KT - 1, KT - 1)
            lo(MLP_U0 + 1, (MLP_U0 + 1) % RAW)
            for k in range(KT):
                k_lo(x1[:, k, :], k, 2 * KT + k, norm2_w[:, k:k + 1])

            def up_low(g, j):
                dve.wait_ge(s_uhi, g * FG + (j + 1))
                dve.wait_ge(s_relu2, g * FG + (j + 1))
                TT(u_lo[:, j, :], relu2[:, :], u_hi[:, j, :].bitcast(F32), ALU.subtract).then_inc(s_ulo, 1)

            def group(g, first, last_):
                for j in range(GU):
                    if j == 0:
                        if not first:
                            dve.wait_ge(s_unit, g * GU + MLP_U0)
                            residual(MLP_T0 + GT - 1, KT - 1)
                    elif j <= 2 * FG:
                        if j % 2 == 0:
                            dve.wait_ge(s_unit, g * GU + (MLP_U0 + j))
                            if first and j == 2:
                                dve.wait_ge(s_n2l, 2)
                            STT(halves(relu[:, (j // 2 - 1) % 2, :]), mains(MLP_T0 + j // 2 - 1), 0.0,
                                halves(rstd[:, :]), ALU.max, ALU.mult).then_inc(s_evac, 1)
                    else:
                        m = j - 2 * FG - 1
                        dve.wait_ge(s_unit, g * GU + (MLP_U0 + j))
                        residual(MLP_T0 + FG + m, m)
                    if not (first and j == 0) and not (last_ and j == GU - 1):
                        lo(g * GU + (MLP_U0 + j + 1), (MLP_U0 + j + 1) % RAW)
                    if j % 2 == 0 and 2 <= j <= 2 * FG:
                        up_low(g, j // 2 - 1)

            group(0, True, False)
            with dve.Fori(1, GROUPS - 1) as g:
                group(g, False, False)
            group(GROUPS - 1, False, True)
            dve.wait_ge(s_unit, MLP_U0 + GU * GROUPS)
            residual(MLP_T0 + GT - 1, KT - 1)
            for m in range(1, KT, 2):
                dve.wait_ge(s_unit, LAST_UP)
                dve.wait_ge(s_fin_pe, m + 1)
                dve.wait_ge(s_fin_copy, m)
                dve.tensor_copy(y[:, :, m * P:m * P + P], wins(2)).then_inc(s_fin_copy, 1)
            dve.wait_ge(s_fw, 16)
            for c in range(NW):
                dve.wait_ge(s_fin, 3 * c + 3)
                STT(y[:, c, :], y[:, c, :], fin[:, c:c + 1], final_w[:, :], ALU.mult, ALU.mult).then_inc(s_fin_dve, 1)


_INS = ["x_prompt", "x_sample", "state_gdn_conv", "state_gdn", "state_hgrn", "meta_tokens", "norm1_w", "w_in", "conv_w",
        "a_log", "dt_bias", "gdn_norm_w", "hgrn_lb", "hgrn_norm_w", "w_out", "norm2_w", "w_up", "w_down",
        "final_norm_w"]
_OUTS = [("y_prompt", (1, NP_, D)), ("y_sample", (SB, ST, D)), ("conv_prompt", (1, 1, PRE, 3 * GK)),
         ("gdn_prompt", (1, 1, HEADS, P, P)), ("hgrn_prompt", (1, 1, HEADS, P, P)),
         ("conv_sample", (1, SB, PRE, 3 * GK)), ("gdn_sample", (1, SB, HEADS, P, P)),
         ("hgrn_sample", (1, SB, HEADS, P, P))]


def kernel(**inputs):
    import numpy as _np
    import concourse.bacc as _bacc
    from concourse.bass_utils import run_bass_kernel_spmd as _run

    nc = _bacc.Bacc("TRN2", target_bir_lowering=False, num_devices=1)
    arrays, io = {}, {}
    for name in _INS:
        a = _np.ascontiguousarray(inputs[name])
        arrays[f"in_{name}"] = a
        io[name] = nc.dram_tensor(f"in_{name}", a.shape, mybir.dt.from_np(a.dtype), kind="ExternalInput").ap()
    for name, shape in _OUTS:
        io[name] = nc.dram_tensor(f"out_{name}", shape, F32, kind="ExternalOutput").ap()
    hymba_kernel(nc, io)
    r = _run(nc, [arrays], core_ids=[0])
    return tuple(r.results[0][f"out_{name}"] for name, _ in _OUTS)
```
